# Optimizing a Trainium2 kernel written in Bass

```python
import math
import jax, jax.numpy as jnp
from jax import lax
import numpy as np

D_MODEL = 1024
BATCH = 1
SEQ = 256
DEPTH = 1
DEC_BATCH = 1
DEC_SEQ = 1024
PAST_LEN = 128

GLA_HEADS = 4
GLA_DK = D_MODEL // 8
GLA_DV = D_MODEL // 4
GLA_QK_W = GLA_HEADS * GLA_DK
GLA_V_W = GLA_HEADS * GLA_DV
GLA_RANK = 16
GLA_TAU = 16.0
GLA_CHUNK = 64

DILATED_GROUPS = ((128, 1), (512, 4), (2048, 16))
N_GROUPS = len(DILATED_GROUPS)
ATT_HEADS = 4
ATT_HD = 128
ATT_W = N_GROUPS * ATT_HEADS * ATT_HD
ATT_OUT_W = ATT_HEADS * ATT_HD
ATT_QBLOCK = 64
NEG_INF = -1e30

D_FF = 4 * D_MODEL
PLE_DIM = 256
RMS_EPS = 1e-6

IN_SIZES = (GLA_QK_W, GLA_QK_W, GLA_V_W, GLA_V_W, GLA_RANK, GLA_RANK,
            ATT_W, ATT_W, ATT_W, D_MODEL, D_MODEL)
D_IN = sum(IN_SIZES)

kernel_name = "hybrid_gla_dilated_attn_encoder"

def _split_points():
    pts, acc = [], 0
    for s in IN_SIZES[:-1]:
        acc += s
        pts.append(acc)
    return pts

def rms_norm(x, g):
    xf = x.astype(jnp.float32)
    y = xf * lax.rsqrt(jnp.mean(xf * xf, axis=-1, keepdims=True) + RMS_EPS)
    return (y * g.astype(jnp.float32)).astype(x.dtype)

def alibi_slopes(n):
    return 2.0 ** (-8.0 * jnp.arange(1, n + 1, dtype=jnp.float32) / n)

def gla_direction(q, k, v, log_a, strict):
    B_, L, H, Dk = q.shape
    Dv = v.shape[-1]
    nc = L // GLA_CHUNK

    def chunks(t):
        return jnp.moveaxis(t.reshape(B_, nc, GLA_CHUNK, H, t.shape[-1]), 1, 0)

    b = jnp.cumsum(chunks(log_a), axis=2)
    tri = jnp.tril(jnp.ones((GLA_CHUNK, GLA_CHUNK), dtype=bool), k=-1 if strict else 0)

    def step(S, inp):
        qc, kc, vc, bc = inp
        qe = qc * jnp.exp(bc)
        ke = kc * jnp.exp(-bc)
        A = jnp.einsum('bthk,bshk->bhts', qe, ke)
        A = jnp.where(tri, A, 0.0)
        o = jnp.einsum('bhts,bshv->bthv', A, vc) + jnp.einsum('bthk,bhkv->bthv', qe, S)
        bl = bc[:, -1]
        S = jnp.exp(bl)[..., None] * S + jnp.einsum(
            'bshk,bshv->bhkv', kc * jnp.exp(bl[:, None] - bc), vc)
        return S, o

    S0 = jnp.zeros((B_, H, Dk, Dv), jnp.float32)
    _, o = lax.scan(step, S0, (chunks(q), chunks(k), chunks(v), b))
    return jnp.moveaxis(o, 0, 1).reshape(B_, L, H, Dv)

def dilated_group(q, k, v, slopes, dilation, half):
    B_, L, H, Dh = q.shape
    Ls = L // dilation
    N = B_ * dilation

    def to_sub(t):
        return t.reshape(B_, Ls, dilation, H, Dh).transpose(0, 2, 1, 3, 4).reshape(N, Ls, H, Dh)

    qs, ks, vs = to_sub(q), to_sub(k), to_sub(v)
    nb = -(-Ls // ATT_QBLOCK)
    Lp = nb * ATT_QBLOCK
    KB = ATT_QBLOCK + 2 * half
    qs = jnp.pad(qs, ((0, 0), (0, Lp - Ls), (0, 0), (0, 0)))
    kpad = ((0, 0), (half, Lp - Ls + half), (0, 0), (0, 0))
    ks = jnp.pad(ks, kpad)
    vs = jnp.pad(vs, kpad)
    qb = qs.reshape(N, nb, ATT_QBLOCK, H, Dh)
    kidx = jnp.arange(nb)[:, None] * ATT_QBLOCK + jnp.arange(KB)[None, :]
    kb = ks[:, kidx]
    vb = vs[:, kidx]
    rel = jnp.arange(ATT_QBLOCK)[:, None] - (jnp.arange(KB)[None, :] - half)
    dist = jnp.abs(rel)
    key_pos = kidx - half
    key_valid = (key_pos >= 0) & (key_pos < Ls)
    mask = (dist <= half)[None] & key_valid[:, None, :]
    s = jnp.einsum('njqhd,njkhd->njhqk', qb, kb) * (Dh ** -0.5)
    s = s - slopes[:, None, None] * (dilation * dist).astype(jnp.float32)[None]
    s = jnp.where(mask[None, :, None], s, NEG_INF)
    lse = jax.nn.logsumexp(s, axis=-1)
    p = jnp.exp(s - lse[..., None])
    o = jnp.einsum('njhqk,njkhd->njqhd', p, vb).reshape(N, Lp, H, Dh)[:, :Ls]
    lse = jnp.swapaxes(lse, 2, 3).reshape(N, Lp, H)[:, :Ls]
    o = o.reshape(B_, dilation, Ls, H, Dh).transpose(0, 2, 1, 3, 4).reshape(B_, L, H, Dh)
    lse = lse.reshape(B_, dilation, Ls, H).transpose(0, 2, 1, 3).reshape(B_, L, H)
    return o, lse

def encoder_layer(x, p, norm_mix_g, w_in, gla_wa2_f, gla_ba_f, gla_wa2_b, gla_ba_b,
                  gla_norm_g, attn_qnorm_g, attn_knorm_g, w_branch_a, w_branch_b, w_out,
                  norm_mlp_g, w_mlp1, w_mlp2, norm_ple_g, w_ple_gate, w_ple_proj):
    B_, L, _ = x.shape
    f32 = jnp.float32
    h = rms_norm(x, norm_mix_g)
    z = h @ w_in
    gq, gk, gv, gg, gaf, gab, aq, ak, av, gate_a, gate_b = jnp.split(z, _split_points(), axis=-1)

    q = gq.reshape(B_, L, GLA_HEADS, GLA_DK).astype(f32)
    k = gk.reshape(B_, L, GLA_HEADS, GLA_DK).astype(f32) * (GLA_DK ** -0.5)
    v = gv.reshape(B_, L, GLA_HEADS, GLA_DV).astype(f32)
    la_f = (jax.nn.log_sigmoid(gaf.astype(f32) @ gla_wa2_f.astype(f32) + gla_ba_f.astype(f32))
            / GLA_TAU).reshape(B_, L, GLA_HEADS, GLA_DK)
    la_b = (jax.nn.log_sigmoid(gab.astype(f32) @ gla_wa2_b.astype(f32) + gla_ba_b.astype(f32))
            / GLA_TAU).reshape(B_, L, GLA_HEADS, GLA_DK)
    o_f = gla_direction(q, k, v, la_f, False)
    o_b = jnp.flip(gla_direction(jnp.flip(q, 1), jnp.flip(k, 1), jnp.flip(v, 1),
                                 jnp.flip(la_b, 1), True), 1)
    o_a = rms_norm(o_f + o_b, gla_norm_g).reshape(B_, L, GLA_V_W)
    o_a = o_a * jax.nn.silu(gg.astype(f32))
    y_a = o_a.astype(x.dtype) @ w_branch_a

    qa = rms_norm(aq.reshape(B_, L, N_GROUPS, ATT_HEADS, ATT_HD).astype(f32),
                  attn_qnorm_g[:, None, :])
    ka = rms_norm(ak.reshape(B_, L, N_GROUPS, ATT_HEADS, ATT_HD).astype(f32),
                  attn_knorm_g[:, None, :])
    va = av.reshape(B_, L, N_GROUPS, ATT_HEADS, ATT_HD).astype(f32)
    slopes = alibi_slopes(N_GROUPS * ATT_HEADS).reshape(N_GROUPS, ATT_HEADS)
    outs, lses = [], []
    for gi, (win, dil) in enumerate(DILATED_GROUPS):
        o_g, lse_g = dilated_group(qa[:, :, gi], ka[:, :, gi], va[:, :, gi], slopes[gi],
                                   dil, win // (2 * dil))
        outs.append(o_g)
        lses.append(lse_g)
    wts = jax.nn.softmax(jnp.stack(lses, 0), axis=0)
    o_att = jnp.sum(wts[..., None] * jnp.stack(outs, 0), axis=0).reshape(B_, L, ATT_OUT_W)
    y_b = o_att.astype(x.dtype) @ w_branch_b

    merged = jax.nn.sigmoid(gate_a) * y_a + jax.nn.sigmoid(gate_b) * y_b
    x = x + merged @ w_out

    h2 = rms_norm(x, norm_mlp_g)
    x = x + jnp.square(jax.nn.relu(h2 @ w_mlp1)) @ w_mlp2

    hp = rms_norm(x, norm_ple_g)
    x = x + jax.nn.sigmoid(hp @ w_ple_gate) * (p @ w_ple_proj)
    return x

def setup_inputs(seed: int = 0) -> dict:
    key = jax.random.key(seed)
    ks = jax.random.split(key, 24)
    f32 = jnp.float32

    def nrm(k, shape, scale):
        return jax.random.normal(k, shape, f32) * scale

    def gain(k, shape):
        return 1.0 + 0.05 * jax.random.normal(k, shape, f32)

    return {
        "x_prompt": nrm(ks[0], (BATCH, SEQ, D_MODEL), 1.0),
        "x_sample": nrm(ks[1], (DEC_BATCH, DEC_SEQ, D_MODEL), 1.0),
        "p_prompt": nrm(ks[2], (DEPTH, BATCH, SEQ, PLE_DIM), 1.0),
        "p_sample": nrm(ks[3], (DEPTH, DEC_BATCH, DEC_SEQ, PLE_DIM), 1.0),
        "norm_mix_g": gain(ks[4], (D_MODEL,)),
        "w_in": nrm(ks[5], (D_MODEL, D_IN), D_MODEL ** -0.5),
        "gla_wa2_f": nrm(ks[6], (GLA_RANK, GLA_QK_W), GLA_RANK ** -0.5),
        "gla_ba_f": nrm(ks[7], (GLA_QK_W,), 0.1),
        "gla_wa2_b": nrm(ks[8], (GLA_RANK, GLA_QK_W), GLA_RANK ** -0.5),
        "gla_ba_b": nrm(ks[9], (GLA_QK_W,), 0.1),
        "gla_norm_g": gain(ks[10], (GLA_DV,)),
        "attn_qnorm_g": gain(ks[11], (N_GROUPS, ATT_HD)),
        "attn_knorm_g": gain(ks[12], (N_GROUPS, ATT_HD)),
        "w_branch_a": nrm(ks[13], (GLA_V_W, D_MODEL), GLA_V_W ** -0.5),
        "w_branch_b": nrm(ks[14], (ATT_OUT_W, D_MODEL), ATT_OUT_W ** -0.5),
        "w_out": nrm(ks[15], (D_MODEL, D_MODEL), D_MODEL ** -0.5),
        "norm_mlp_g": gain(ks[16], (D_MODEL,)),
        "w_mlp1": nrm(ks[17], (D_MODEL, D_FF), D_MODEL ** -0.5),
        "w_mlp2": nrm(ks[18], (D_FF, D_MODEL), D_FF ** -0.5),
        "norm_ple_g": gain(ks[19], (D_MODEL,)),
        "w_ple_gate": nrm(ks[20], (D_MODEL, D_MODEL), D_MODEL ** -0.5),
        "w_ple_proj": nrm(ks[21], (PLE_DIM, D_MODEL), PLE_DIM ** -0.5),
    }

def reference(x_prompt, x_sample, p_prompt, p_sample, norm_mix_g, w_in, gla_wa2_f, gla_ba_f,
              gla_wa2_b, gla_ba_b, gla_norm_g, attn_qnorm_g, attn_knorm_g, w_branch_a,
              w_branch_b, w_out, norm_mlp_g, w_mlp1, w_mlp2, norm_ple_g, w_ple_gate,
              w_ple_proj):
    y_prompt = x_prompt
    y_sample = x_sample
    for i in range(DEPTH):
        y_prompt = encoder_layer(y_prompt, p_prompt[i], norm_mix_g, w_in, gla_wa2_f, gla_ba_f,
                                 gla_wa2_b, gla_ba_b, gla_norm_g, attn_qnorm_g, attn_knorm_g,
                                 w_branch_a, w_branch_b, w_out, norm_mlp_g, w_mlp1, w_mlp2,
                                 norm_ple_g, w_ple_gate, w_ple_proj)
        y_sample = encoder_layer(y_sample, p_sample[i], norm_mix_g, w_in, gla_wa2_f, gla_ba_f,
                                 gla_wa2_b, gla_ba_b, gla_norm_g, attn_qnorm_g, attn_knorm_g,
                                 w_branch_a, w_branch_b, w_out, norm_mlp_g, w_mlp1, w_mlp2,
                                 norm_ple_g, w_ple_gate, w_ple_proj)
    return (y_prompt, y_sample)


_drawn_inputs = setup_inputs


def setup_inputs(seed=0):
    import zlib

    import numpy as np

    out = dict(_drawn_inputs(seed))
    spreads = {}
    factors = {'gla_ba_f': 5.698,
     'gla_ba_b': 5.756,
     'gla_norm_g': 3.433,
     'attn_qnorm_g': 8.0,
     'attn_knorm_g': 8.0,
     'norm_ple_g': 26.935}
    for name, (base, spread) in spreads.items():
        noise = np.random.default_rng([zlib.crc32(name.encode()), seed]).standard_normal(out[name].shape)
        drawn = base * np.exp(spread * noise) if base else spread * noise
        out[name] = __import__('jax').numpy.asarray(drawn.astype(out[name].dtype))
    for name, factor in factors.items():
        out[name] = (out[name] * factor).astype(out[name].dtype)
    return out
```

```python
from contextlib import ExitStack

import concourse.bass as bass
from concourse import mybir

ALU = mybir.AluOpType
ACT = mybir.ActivationFunctionType
F32 = mybir.dt.float32
FR = mybir.dt.float32r
U8 = mybir.dt.uint8
I32 = mybir.dt.int32
P = 128

MAP_BYTES = 212736
EPS = 1e-6
MASKED = 1e32


class Chain:

    def __init__(self):
        self.n, self.base = 0, 0

    def value(self):
        self.n += 1
        return self.base + self.n + 1

    def enter(self, i, per):
        self.before, self.per, self.n = self.n, per, 0
        self.base = self.base + self.before + i * per

    def leave(self, times, start):
        assert self.n == self.per, (self.n, self.per)
        self.base, self.n = start + times * self.per, 0


def encoder(nc, a, out_p, out_s):
    D = a["x_sample"].shape[2]
    TS, TP = a["x_sample"].shape[1], a["x_prompt"].shape[1]
    T = TS + TP
    KT = D // P
    NT = T // P
    H = 4
    DK, DV = 128, 256
    RANK = a["gla_wa2_f"].shape[0]
    CHUNKS = [(0, 512), (512, 512), (1024, 256)]
    FF = a["w_mlp1"].shape[1]
    PLE = a["p_sample"].shape[3]
    BLK = NT
    C_GQ = 0
    C_GK = C_GQ + H * DK
    C_GV = C_GK + H * DK
    C_GG = C_GV + H * DV
    C_LR = C_GG + H * DV
    C_AQ = C_LR + 2 * RANK
    C_AK = C_AQ + 3 * H * P
    C_AV = C_AK + 3 * H * P
    C_GATE = C_AV + 3 * H * P
    SLOTS = 18
    N_HEAD = 1
    N_REST = N_HEAD + H * SLOTS
    REST = 2 * KT - 3 * H
    N_C1 = N_REST + REST
    N_C2 = N_C1 + 2 * KT
    N_D = N_C2 + KT
    ROUNDS = FF // (2 * P)
    N_E = N_D + 4 * ROUNDS

    def slab_chunks(n):
        return 3 * n

    with ExitStack() as ctx:
        first = {}

        def sem(name, start=1):
            s = ctx.enter_context(nc.semaphore(name))
            first[s] = start
            return s

        base = (nc.sbuf_base + 31) // 32 * 32
        ctx.enter_context(nc.sbuf_tensor("whole_map", [P, MAP_BYTES // 4], F32))
        ROW = T * 4
        O_HLO = KT * ROW
        O_WHI = 2 * KT * ROW
        O_WLO = O_WHI + 8192
        O_RAW = O_WLO + 8192
        O_WORK = O_RAW + 4096
        O_SMALL = O_WORK + 18 * ROW

        def at(name, shape, dt, off):
            return nc.alloc_sbuf_tensor_at(name, shape, dt, offset=base + off)

        act_hi = at("act_hi", [P, KT, T], FR, 0)
        act_lo = at("act_lo", [P, KT, T], FR, O_HLO)
        w_hi = at("w_hi", [P, 2, 1024], FR, O_WHI)
        w_lo = at("w_lo", [P, 2, 1024], FR, O_WLO)
        w_raw = at("w_raw", [P, 1024], F32, O_RAW)
        work = at("work", [P, 18, T], F32, O_WORK)
        z = work[:, 0:6, :]
        ar = work[:, 6:18, :]
        x_in = at("x_in", [P, NT, 1024], F32, O_WORK)
        x_sq = at("x_sq", [P, 1024], F32, O_WORK + 8 * ROW)
        ob_hi = at("ob_hi", [P, 4, T], FR, O_WORK)
        ob_lo = at("ob_lo", [P, 4, T], FR, O_WORK + 4 * ROW)
        merged = work[:, 8:16, :]
        xres = work[:, 0:8, :]
        u_hi = at("u_hi", [P, 2, T], FR, O_WORK + 8 * ROW)
        u_lo = at("u_lo", [P, 2, T], FR, O_WORK + 10 * ROW)
        pos = [O_SMALL]

        def small(name, shape, dt=F32):
            size = 1
            for s in shape[1:]:
                size *= s
            size *= 1 if dt == U8 else 4
            t = at(name, shape, dt, pos[0])
            pos[0] += (size + 31) // 32 * 32
            return t

        shared = pos[0]
        pr = at("pr", [P, 2, 256], F32, shared)
        prt = at("prt", [P, 2, 256], F32, shared + 2048)
        bias_w = at("bias_w", [P, 256], F32, shared + 4096)
        bias_b = at("bias_b", [P, P], F32, shared + 5120)
        amat = at("amat", [P, 2, P], F32, shared)
        kdn = at("kdn", [P, 2, 2, P], F32, shared + 1024)
        state = at("state", [P, 2, 2, DV], F32, shared + 3072)
        utmp = at("utmp", [P, 2, 512], F32, shared)
        pos[0] = shared + 7168
        dist_w = small("dist_w", [P, 256])
        dist_2 = small("dist_2", [P, P])
        dist_8 = small("dist_8", [P, P])
        ident = small("ident", [P, P])
        ones = small("ones", [P, P])
        mask_f = small("mask_f", [P, P], U8)
        mask_b = small("mask_b", [P, P], U8)
        r_bc = at("r_bc", [P, T], F32, pos[0])
        lowrank = small("lowrank", [48, T])
        wa2 = small("wa2", [48, DK])
        ba = small("ba", [P, 2])
        st = small("st", [P, 2 * BLK])
        st_t = small("st_t", [2 * BLK, P])
        cst = small("cst", [P, 6, NT])
        cw = small("cw", [P, 4, NT])
        ebl = small("ebl", [P, 2, T // 64])
        slopes = small("slopes", [P, 3 * H])
        slope = small("slope", [P, 3])
        g_mix = small("g_mix", [P, KT])
        g_mlp = small("g_mlp", [P, KT])
        g_ple = small("g_ple", [P, KT])
        g_gla = small("g_gla", [P, 2])
        g_q = small("g_q", [P, 3])
        g_k = small("g_k", [P, 3])
        eps = small("eps", [P, 1])
        half = small("half", [P, 4])
        ssx = small("ssx", [P, NT])
        rx = small("rx", [P, NT])
        assert pos[0] <= MAP_BYTES, pos[0]

        bank = [ctx.enter_context(nc.psum_tensor(f"bank{i}", [P, 512], F32)) for i in range(8)]

        def dram(name, shape):
            return nc.dram_tensor(name, shape, F32, kind="Internal").ap()

        oa_d = dram("oa_scratch", [H * DV, T])
        ob_d = dram("ob_scratch", [H * P, T])
        gate_d = dram("gate_scratch", [2 * D, T])
        stat_d = dram("stat_scratch", [2, 3, T])
        wgt_d = dram("weight_scratch", [3, T])
        unused_d = dram("unused_scratch", [D])

        w_in = a["w_in"].rearrange("(k p) n -> p k n", p=P)
        w_a = a["w_branch_a"].rearrange("(k p) n -> p k n", p=P)
        w_b = a["w_branch_b"].rearrange("(k p) n -> p k n", p=P)
        w_o = a["w_out"].rearrange("(k p) n -> p k n", p=P)
        w_1 = a["w_mlp1"].rearrange("(k p) n -> p k n", p=P)
        w_2 = a["w_mlp2"].rearrange("(f k p) n -> p f k n", p=P, k=2)
        w_pg = a["w_ple_gate"].rearrange("(k p) n -> p k n", p=P)
        w_pp = a["w_ple_proj"].rearrange("(k p) n -> p k n", p=P)
        x_s = a["x_sample"].rearrange("o t d -> (o t) d")
        x_p = a["x_prompt"].rearrange("o t d -> (o t) d")
        p_s = a["p_sample"].rearrange("l o t d -> (l o t) d")
        p_p = a["p_prompt"].rearrange("l o t d -> (l o t) d")
        y_s = out_s.rearrange("o t d -> (o t) d")
        y_p = out_p.rearrange("o t d -> (o t) d")

        primed = sem("primed")
        const_dma = sem("const_dma", 0)
        ident_ready = sem("ident_ready", 0)
        const_pool = sem("const_pool")
        const_dve = sem("const_dve")
        pool_own, dve_own, act_own = sem("pool_own"), sem("dve_own"), sem("act_own")
        sp_passed, pool_passed, act_passed, dve_passed = (
            sem("sp_passed"), sem("pool_passed"), sem("act_passed"), sem("dve_passed"))
        w_zero = sem("w_zero", 0)
        w_loaded = sem("w_loaded", 0)
        w_high = sem("w_high")
        w_split = sem("w_split")
        mm_done = sem("mm_done")
        evac = sem("evac")
        x_loaded = [sem(f"x_loaded{t}", 0) for t in range(NT)]
        x_sumsq, x_r, x_norm, x_tr, x_high, x_low = (
            sem("x_sumsq", 0), sem("x_r", 0), sem("x_norm", 0), sem("x_tr", 0), sem("x_high", 0), sem("x_low", 0))
        sq_ready, ss_done, ln_done, r_ready, qk_ready = (
            sem("sq_ready"), sem("ss_done"), sem("ln_done"), sem("r_ready"), sem("qk_ready"))
        vt_done, vn_ready = sem("vt_done"), sem("vn_ready")
        bias_ready = sem("bias_ready")
        scores_done, max_done, exp_done = sem("scores_done"), sem("max_done"), sem("exp_done")
        prt_done, prt_read, pv_done, o_read = sem("prt_done"), sem("prt_read"), sem("pv_done"), sem("o_read")
        stt_done, stt_read, stat_stored = sem("stt_done"), sem("stt_read"), sem("stat_stored", 16)
        cst_loaded, cexp_in, cexp_out, cw_ready = sem("cst_loaded", 0), sem("cexp_in"), sem("cexp_out"), sem("cw_ready")
        cw_stored, wb_loaded, ob_ready, ob_stored = sem("cw_stored", 16), sem("wb_loaded", 0), sem("ob_ready"), sem("ob_stored", 0)
        gate_stored = sem("gate_stored", 16)
        rest_stored = [sem("rest_stored0", 0), sem("rest_stored1", 0)]
        carry_ready = sem("carry_ready")
        i0_done = sem("i0_done")
        head_loaded = sem("head_loaded", 0)
        lr_done, y_read, prep_a, prep_d = sem("lr_done"), sem("y_read"), sem("prep_a"), sem("prep_d")
        gvt_done, gvn_ready = sem("gvt_done"), sem("gvn_ready")
        pre_done, kdn_ready, a_ready = sem("pre_done"), sem("kdn_ready"), sem("a_ready")
        u_done, s_ready, o_done, go_copied, go_added = (
            sem("u_done"), sem("s_ready"), sem("o_done"), sem("go_copied"), sem("go_added"))
        osq_ready, oss_done, gate_ready, head_done, oa_stored = (
            sem("osq_ready"), sem("oss_done"), sem("gate_ready"), sem("head_done"), sem("oa_stored", 16))
        ob_loaded, oa_loaded = sem("ob_loaded", 0), sem("oa_loaded", 0)
        c_high, c_low = sem("c_high"), sem("c_low")
        g_loaded, g_sig = sem("g_loaded", 0), sem("g_sig")
        yb_done, yb_read, m_done = sem("yb_done"), sem("yb_read"), sem("m_done")
        m_high, m_low = sem("m_high"), sem("m_low")
        xn_loaded = [sem("xn_loaded0", 0), sem("xn_loaded1", 0)]
        x1_sq, x1_acc, x1_ss, n_ln, n_r, n_high, n_low = (
            sem("x1_sq"), sem("x1_acc"), sem("x1_ss"), sem("n_ln"), sem("n_r"), sem("n_high"), sem("n_low"))
        u_act, u_sq, u_high, u_low = sem("u_act"), sem("u_sq"), sem("u_high"), sem("u_low")
        w2_done, w2_read = sem("w2_done"), sem("w2_read")
        p_loaded, p_tr, p_high, p_low = sem("p_loaded", 0), sem("p_tr"), sem("p_high"), sem("p_low")
        pg_r, pg_sig, pp_done, y_ready, yt_done, yt_read, y_stored = (
            sem("pg_r"), sem("pg_sig"), sem("pp_done"), sem("y_ready"), sem("yt_done"), sem("yt_read"), sem("y_stored", 16))

        def seqs(row):
            return row[:, 0:TS], row[:, TS:T]

        def queries(row, g, b):
            s, p = seqs(row)
            if g == 0:
                return s[:, P * b:P * b + P] if b < 8 else p[:, P * (b - 8):P * (b - 7)]
            if g == 1:
                if b < 8:
                    return s.rearrange("p (l r) -> p r l", r=4)[:, b % 4, P * (b // 4):P * (b // 4) + P]
                return p.rearrange("p (l r) -> p r l", r=4)[:, 2 * (b - 8):2 * (b - 7), :]
            if b < 8:
                return s.rearrange("p (l r) -> p r l", r=16)[:, 2 * b:2 * b + 2, :]
            return p.rearrange("p (l r) -> p r l", r=16)[:, 8 * (b - 8):8 * (b - 7), :]

        def window(g, b):
            if g == 0:
                ln, l0 = (TS, P * b) if b < 8 else (TP, P * (b - 8))
            elif g == 1 and b < 8:
                ln, l0 = TS // 4, P * (b // 4)
            else:
                return None
            return l0, max(0, l0 - 64), min(ln, l0 + 192), ln

        def block_at(g, b):
            return TS // 4 * (b % 4) + P * (b // 4) if g == 1 and b < 8 else P * b

        def keys(row, g, b):
            w = window(g, b)
            if w is None:
                return row[:, P * b:P * b + P]
            seq = (0 if b < 8 else TS) if g == 0 else TS // 4 * (b % 4)
            return row[:, seq + w[1]:seq + w[2]]

        def by_residue(row, g, c):
            dil = (1, 4, 16)[g]
            s, p = seqs(row)
            if c == 2:
                return p.rearrange("p (r l) -> p r l", r=dil)
            n = 512 // dil
            return s.rearrange("p (r l) -> p r l", r=dil)[:, :, c * n:c * n + n]

        def value_tile(g, m):
            if g == 0 and m in (0, 8):
                s0, s1 = (0, TS) if m == 0 else (TS, T)
            elif g == 1 and m < 8 and m % 2 == 0:
                s0, s1 = TS // 4 * (m // 2), TS // 4 * (m // 2 + 1)
            elif g == 0:
                return [(P * m - 64, P * m + 64)]
            elif g == 1 and m < 8:
                return [(TS // 4 * (m // 2) + 64, TS // 4 * (m // 2) + 192)]
            else:
                return [(P * m, P * m + P)]
            return [(s1 - P, s1), (s0, s0 + 64)]

        def pieces(g, b):
            w = window(g, b)
            if w is None:
                return [(b, 0, P, 0)]
            l0, lo, hi, ln = w
            if g == 0:
                edge, mid = (0, b) if b < 8 else (8, 9)
                before, behind = (mid, mid + 1) if b < 8 else (9, 9)
            else:
                edge = 2 * (b % 4)
                before = behind = edge + 1
            if l0 == 0:
                return [(edge, 0, 64, 0), (behind, 0, P, 64)]
            if hi == ln:
                return [(before, 0, P, 0), (edge, 64, P, 64)]
            return [(before, 0, P, 0), (behind, 0, P, P)]

        def like(flat, shaped):
            if len(shaped.shape) == 3:
                return flat.rearrange("p (j l) -> p j l", j=shaped.shape[1])
            return flat

        WB = (6, 7, 9)
        carry = ar[:, 8, :].rearrange("p (c l) -> p c l", l=64)
        keyvals = work[:, 12:14, :].rearrange("p a t -> p (a t)").rearrange("p (n v) -> p n v", v=DV)
        o_gla = ar[:, 8:10, :]
        BSTEP = 4
        T_STAT = 19 + BSTEP * BLK + 1
        T_LR = (281, 300)
        T_DECAY = (290, 331)
        T_QK = (294, 337)
        T_CW = 285
        T_COMBINE = 305
        T_VT = 321
        T_GLA, GSTEP = 351, 7
        X_TILES = [(t0 // P, (t0 + tw) // P) for t0, tw in CHUNKS]
        Z_OF = [0, 1, 2, 3, 4, 5, 0, 1, 2, 3, 4, 5, 0, 1, 2, 3, 4, 5]

        ctx.enter_context(nc.allow_non_contiguous_dma(reason="small vectors and softmax statistics"))
        block = ctx.enter_context(nc.Block())

        @block.sync
        def _(sp):
            def load(n, src, width=1024, first=False):
                if not first:
                    sp.wait_ge(w_split, n + 1)
                    sp.sem_inc(sp_passed, 1)
                sp.dma_start(w_raw[:, 0:width].rearrange("p (k n) -> p k n", n=src.shape[2]), src).then_inc(w_loaded, 16)

            for t in range(NT):
                src, row = (x_s, t * P) if t < TS // P else (x_p, t * P - TS)
                sp.dma_start(x_in[:, t, :], src[row:row + P, :]).then_inc(x_loaded[t], 16)
            sp.wait_ge(primed, 1)
            with sp.Fori(0, H) as h:
                n = N_HEAD + h * SLOTS
                cols = []
                for g in range(3):
                    cols += [C_AK + g * H * P + h * P, C_AQ + g * H * P + h * P, C_AV + g * H * P + h * P]
                cols += [C_GK + h * DK, C_GQ + h * DK, C_GV + h * DV, C_GV + P + h * DV, C_GG + h * DV, C_GG + P + h * DV]
                cols += [C_GATE + j * P + h * (3 * P) for j in range(3)]
                for t, c in enumerate(cols):
                    load(n + t, w_in[:, :, bass.ds(c, P)])
            for j in range(REST):
                c = C_GATE + (3 * H + j) * P
                load(N_REST + j, w_in[:, :, c:c + P])
            with sp.Fori(0, KT) as j:
                load(N_C1 + 2 * j, w_a[:, :, bass.ds(j * P, P)])
                load(N_C1 + 1 + 2 * j, w_b[:, :, bass.ds(j * P, P)], 512)
            with sp.Fori(0, KT) as j:
                load(N_C2 + j, w_o[:, :, bass.ds(j * P, P)])
            with sp.Fori(0, ROUNDS) as i:
                for e in range(2):
                    load(N_D + e + 4 * i, w_1[:, :, bass.ds(i * (2 * P) + e * P, P)])
                for e in range(2):
                    load(N_D + 2 + e + 4 * i, w_2[:, i, :, 512 * e:512 * e + 512])
            with sp.Fori(0, KT) as j:
                load(N_E + 2 * j, w_pg[:, :, bass.ds(j * P, P)])
                load(N_E + 1 + 2 * j, w_pp[:, :, bass.ds(j * P, P)], 256)

        @block.gpsimd
        def _(pool):
            own = Chain()
            nc.gpsimd.memset(ident[:], 0.0).then_inc(ident_ready, 1)
            pool.wait_ge(ident_ready, 1)
            nc.gpsimd.affine_select(out=ident[:], in_=ident[:], compare_op=ALU.not_equal, fill=1.0, base=0,
                                    pattern=[[-1, P]], channel_multiplier=1).then_inc(ident_ready, 1)
            for i, (s, start) in enumerate(first.items()):
                if start == 1 and s is not primed:
                    pool.sem_inc(s, 1)
                if start == 16:
                    pool.dma_start(unused_d[i:i + 1], a["norm_mix_g"][0:1]).then_inc(s, 16)
            for s, start in first.items():
                if start == 16:
                    pool.wait_ge(s, 16)
            pool.sem_inc(primed, 1)
            nc.gpsimd.memset(eps[:], EPS).then_inc(pool_own, 1)
            pool.wait_ge(pool_own, own.value())
            nc.gpsimd.memset(half[:], -0.5).then_inc(pool_own, 1)
            pool.wait_ge(pool_own, own.value())
            for t0, t1 in X_TILES:
                pool.wait_ge(x_sumsq, t1)
                nc.gpsimd.tensor_scalar(rx[:, t0:t1], ssx[:, t0:t1], 1.0 / D, EPS, ALU.mult, ALU.add).then_inc(pool_own, 1)
                pool.wait_ge(pool_own, own.value())
                nc.gpsimd.tensor_tensor(rx[:, t0:t1], rx[:, t0:t1], half[:, 0:t1 - t0], ALU.pow).then_inc(x_r, 1)

            for k in range(3 * H):
                nc.gpsimd.memset(slopes[:, k:k + 1], 2.0 ** (-8.0 * (k % 3 * H + k // 3 + 1) / (3 * H)) * (1, 4, 16)[k % 3]).then_inc(pool_own, 1)
                pool.wait_ge(pool_own, own.value())
                pool.sem_inc(pool_passed, 1)
            iot = ar[:, 11, 0:256]
            neg = ar[:, 11, 256:512]

            def distance(first):
                nc.gpsimd.iota(iot, [[1, 256]], base=first, channel_multiplier=-1, allow_small_or_imprecise_dtypes=True).then_inc(pool_own, 1)
                pool.wait_ge(pool_own, own.value())
                pool.sem_inc(pool_passed, 1)
                nc.gpsimd.tensor_scalar(neg, iot, -1.0, None, ALU.mult).then_inc(pool_own, 1)
                pool.wait_ge(pool_own, own.value())
                pool.sem_inc(pool_passed, 1)
                nc.gpsimd.affine_select(out=iot, in_=iot, compare_op=ALU.is_ge, fill=0.0, base=first,
                                        pattern=[[1, 256]], channel_multiplier=-1).then_inc(pool_own, 1)
                pool.wait_ge(pool_own, own.value())
                pool.sem_inc(pool_passed, 1)
                nc.gpsimd.affine_select(out=neg, in_=neg, compare_op=ALU.is_ge, fill=0.0, base=-first,
                                        pattern=[[-1, 256]], channel_multiplier=1).then_inc(pool_own, 1)
                pool.wait_ge(pool_own, own.value())
                pool.sem_inc(pool_passed, 1)

            distance(-64)
            nc.gpsimd.tensor_tensor(dist_w[:], iot, neg, ALU.add).then_inc(pool_own, 1)
            pool.wait_ge(pool_own, own.value())
            pool.sem_inc(pool_passed, 1)
            nc.gpsimd.affine_select(out=dist_w[:], in_=dist_w[:], compare_op=ALU.is_ge, fill=MASKED, base=128,
                                    pattern=[[-1, 256]], channel_multiplier=1).then_inc(pool_own, 1)
            pool.wait_ge(pool_own, own.value())
            pool.sem_inc(pool_passed, 1)
            nc.gpsimd.affine_select(out=dist_w[:], in_=dist_w[:], compare_op=ALU.is_ge, fill=MASKED, base=0,
                                    pattern=[[1, 256]], channel_multiplier=-1).then_inc(pool_own, 1)
            pool.wait_ge(pool_own, own.value())
            pool.sem_inc(pool_passed, 1)
            distance(0)
            for dst, w in ((dist_2, 64), (dist_8, 16)):
                nc.gpsimd.tensor_tensor(dst[:], iot[:, 0:P], neg[:, 0:P], ALU.add).then_inc(pool_own, 1)
                pool.wait_ge(pool_own, own.value())
                pool.sem_inc(pool_passed, 1)
                v = dst[:].rearrange("p (j l) -> p j l", l=w)
                nc.gpsimd.affine_select(out=v, in_=v, compare_op=ALU.is_ge, fill=MASKED, base=0,
                                        pattern=[[-w, P // w], [0, w]], channel_multiplier=1).then_inc(pool_own, 1)
                pool.wait_ge(pool_own, own.value())
                pool.sem_inc(pool_passed, 1)
                nc.gpsimd.affine_select(out=v, in_=v, compare_op=ALU.is_ge, fill=MASKED, base=w - 1,
                                        pattern=[[w, P // w], [0, w]], channel_multiplier=-1).then_inc(pool_own, 1)
                pool.wait_ge(pool_own, own.value())
                pool.sem_inc(pool_passed, 1)
            for msk, cmp_, sign in ((mask_f, ALU.is_ge, 1), (mask_b, ALU.is_gt, -1)):
                m = ar[:, 11, 512:640]
                v = m.rearrange("p (j l) -> p j l", l=64)
                nc.gpsimd.memset(m, 1.0).then_inc(pool_own, 1)
                pool.wait_ge(pool_own, own.value())
                pool.sem_inc(pool_passed, 1)
                nc.gpsimd.affine_select(out=v, in_=v, compare_op=ALU.is_ge, fill=0.0, base=0,
                                        pattern=[[-64, 2], [0, 64]], channel_multiplier=1).then_inc(pool_own, 1)
                pool.wait_ge(pool_own, own.value())
                pool.sem_inc(pool_passed, 1)
                nc.gpsimd.affine_select(out=v, in_=v, compare_op=ALU.is_ge, fill=0.0, base=63,
                                        pattern=[[64, 2], [0, 64]], channel_multiplier=-1).then_inc(pool_own, 1)
                pool.wait_ge(pool_own, own.value())
                pool.sem_inc(pool_passed, 1)
                nc.gpsimd.affine_select(out=m, in_=m, compare_op=cmp_, fill=0.0, base=0,
                                        pattern=[[sign, P]], channel_multiplier=-sign).then_inc(pool_own, 1)
                pool.wait_ge(pool_own, own.value())
                pool.sem_inc(pool_passed, 1)
                nc.gpsimd.tensor_copy(msk[:], m).then_inc(pool_own, 1)
                pool.wait_ge(pool_own, own.value())
                pool.sem_inc(pool_passed, 1)
            pool.sem_inc(const_pool, 1)

            def store_gate(n, zrow, rows, stored):
                pool.wait_ge(evac, slab_chunks(n + 1) + 1)
                pool.sem_inc(pool_passed, 1)
                pool.dma_start(gate_d[rows, :], work[:, zrow, :]).then_inc(stored, 16)

            def store_stats(h, g):
                pool.wait_ge(stt_read, 3 * h + g + 2)
                pool.sem_inc(pool_passed, 1)
                for mz in range(2):
                    r0 = mz * BLK
                    s = stat_d[mz, g, 0:TS]
                    p = stat_d[mz, g, TS:T]
                    if g == 0:
                        todo = [(st_t[r0:r0 + 10, :], stat_d[mz, g, :].rearrange("(b q) -> b q", q=P))]
                    elif g == 1:
                        sv = s.rearrange("(f l r) -> f r l", r=4, l=P)
                        todo = [(st_t[r0 + 4 * f:r0 + 4 * f + 4, :], sv[f]) for f in range(2)]
                        todo.append((st_t[r0 + 8:r0 + 10, :].rearrange("b (j l) -> b j l", j=2),
                                     p.rearrange("(l b j) -> b j l", b=2, j=2)))
                    else:
                        todo = [(st_t[r0:r0 + 8, :].rearrange("b (j l) -> b j l", j=2),
                                 s.rearrange("(l b j) -> b j l", b=8, j=2)),
                                (st_t[r0 + 8:r0 + 10, :].rearrange("b (j l) -> b j l", j=8),
                                 p.rearrange("(l b j) -> b j l", b=2, j=8))]
                    for src, dst in todo:
                        pool.dma_start(dst, src).then_inc(stat_stored, 16)

            start = own.base + own.n
            with pool.Fori(0, H) as h:
                own.enter(h, 2)
                pool.wait_ge(head_done, h + 1)
                pool.sem_inc(pool_passed, 1)
                for d, (w2, b2) in enumerate((("gla_wa2_f", "gla_ba_f"), ("gla_wa2_b", "gla_ba_b"))):
                    pool.dma_start(wa2[32 * d:32 * d + RANK, :], a[w2][:, bass.ds(h * DK, DK)]).then_inc(head_loaded, 16)
                    pool.dma_start(ba[:, d:d + 1], a[b2].rearrange("(n o) -> n o", o=1)[bass.ds(h * DK, DK), :]
                                   ).then_inc(head_loaded, 16)
                pool.wait_ge(oa_stored, 32 * h + 16)
                pool.sem_inc(pool_passed, 1)
                nc.gpsimd.memset(ar[:, 8, :], 1.0).then_inc(pool_own, 1)
                pool.wait_ge(pool_own, own.value())
                pool.sem_inc(pool_passed, 1)
                nc.gpsimd.memset(carry[:, :, 0:1], 0.0).then_inc(carry_ready, 1)
                for g in range(3):
                    store_stats(h, g)
                pool.wait_ge(stat_stored, 16 * 12 * (h + 1) + 16)
                pool.sem_inc(pool_passed, 1)
                pool.dma_start(cst[:], stat_d.rearrange("m g (p j) -> p (m g) j", j=NT)).then_inc(cst_loaded, 16)
                pool.wait_ge(prep_d, 8 * h + 3)
                pool.sem_inc(pool_passed, 1)
                nc.gpsimd.memset(carry[:, :, 0:1], 1.0).then_inc(pool_own, 1)
                pool.wait_ge(pool_own, own.value())
                pool.sem_inc(pool_passed, 1)
                nc.gpsimd.memset(carry[:, :, 63:64], 0.0).then_inc(carry_ready, 1)
                pool.wait_ge(cw_ready, h + 2)
                pool.sem_inc(pool_passed, 1)
                pool.dma_start(wgt_d.rearrange("g (p j) -> p g j", j=NT), cw[:, 0:3, :]).then_inc(cw_stored, 16)
                pool.wait_ge(cw_stored, 16 * (h + 1) + 16)
                pool.sem_inc(pool_passed, 1)
                for g in range(3):
                    pool.dma_start(ar[:, WB[g], :], wgt_d[g, :].partition_broadcast(P)).then_inc(wb_loaded, 16)
                pool.wait_ge(ob_ready, h + 2)
                pool.sem_inc(pool_passed, 1)
                pool.dma_start(ob_d[bass.ds(h * P, P), :], ar[:, 3, :]).then_inc(ob_stored, 16)
                for j in range(3):
                    store_gate(N_HEAD + h * SLOTS + 15 + j, Z_OF[15 + j], bass.ds(h * (3 * P) + j * P, P), gate_stored)
                pool.wait_ge(head_done, h + 2)
                pool.sem_inc(pool_passed, 1)
                for v in range(2):
                    pool.dma_start(oa_d[bass.ds(h * DV + v * P, P), :], ar[:, 8 + v, :]).then_inc(oa_stored, 16)
            own.leave(H, start)

            pool.wait_ge(oa_stored, 32 * H + 16)
            pool.sem_inc(pool_passed, 1)
            pool.wait_ge(ob_stored, 16 * H)
            pool.sem_inc(pool_passed, 1)
            for k in range(KT):
                pool.dma_start(merged[:, k, :], oa_d[P * k:P * k + P, :]).then_inc(oa_loaded, 16)
            pool.wait_ge(gate_stored, 16 * 3 * H + 16)
            pool.sem_inc(pool_passed, 1)
            for k in range(4):
                pool.dma_start(work[:, 4 + k, :], ob_d[P * k:P * k + P, :]).then_inc(ob_loaded, 16)
            for j in range(REST):
                rows = slice((3 * H + j) * P, (3 * H + j + 1) * P)
                store_gate(N_REST + j, 16 + j % 2, rows, rest_stored[j % 2])
            for e in range(2):
                pool.wait_ge(rest_stored[e], 16 * REST // 2)
                pool.sem_inc(pool_passed, 1)
            with pool.Fori(0, KT) as j:
                pool.wait_ge(m_done, 3 * j + 1)
                pool.sem_inc(pool_passed, 1)
                for e in range(2):
                    pool.dma_start(work[:, 16 + e, :], gate_d[bass.ds(j * P + e * D, P), :]).then_inc(g_loaded, 16)

            def load_x(j, e):
                pool.wait_ge(mm_done, slab_chunks(N_C2 - 1 + e) + 6 * j + 1)
                pool.sem_inc(pool_passed, 1)
                dst = work[:, 16 + e, :].rearrange("p (n d) -> p n d", d=P)
                cols = bass.ds(j * (2 * P) + e * P, P)
                pool.dma_start(dst[:, 0:TS // P, :], x_s.rearrange("(n p) d -> p n d", p=P)[:, :, cols]).then_inc(xn_loaded[e], 16)
                pool.dma_start(dst[:, TS // P:NT, :], x_p.rearrange("(n p) d -> p n d", p=P)[:, :, cols]).then_inc(xn_loaded[e], 16)

            pool.wait_ge(m_done, 3 * KT + 1)
            pool.sem_inc(pool_passed, 1)
            with pool.Fori(0, KT // 2) as j:
                for e in range(2):
                    load_x(j, e)

            pool.wait_ge(x1_ss, 2)
            pool.sem_inc(pool_passed, 1)
            for e in range(2):
                dst = work[:, 12 + e, :].rearrange("p (n d) -> p n d", d=P)
                for src, n0, n1 in ((p_s, 0, TS // P), (p_p, TS // P, NT)):
                    pool.dma_start(dst[:, n0:n1, :], src.rearrange("(n p) d -> p n d", p=P)[:, :, e * P:e * P + P]
                                   ).then_inc(p_loaded, 16)
            with pool.Fori(0, KT) as j:
                pool.wait_ge(yt_read, 3 * j + 4)
                pool.sem_inc(pool_passed, 1)
                src = work[:, 16, :].rearrange("p (n d) -> p n d", d=P)
                cols = bass.ds(j * P, P)
                for dst, n0, n1 in ((y_s, 0, TS // P), (y_p, TS // P, NT)):
                    pool.dma_start(dst.rearrange("(n p) d -> p n d", p=P)[:, :, cols], src[:, n0:n1, :]
                                   ).then_inc(y_stored, 16)
            pool.wait_ge(y_stored, 32 * KT + 16)
            pool.sem_inc(pool_passed, 1)

        @block.tensor
        def _(pe):
            def ready(n, c):
                if c == 0:
                    pe.wait_ge(w_split, n + 2)
                pe.wait_ge(evac, slab_chunks(n - 1) + c + 2)

            def steps(slot, c, k0, k1, kt, hi, lo, out=None, first=True, column=lambda k: k):
                t0, tw = CHUNKS[c]
                out = bank[c][:, 0:tw] if out is None else out
                for k in range(k0, k1):
                    w0 = column(k) * P
                    wh, wl = w_hi[:, slot, w0:w0 + P], w_lo[:, slot, w0:w0 + P]
                    rh, rl = hi[:, k, t0:t0 + tw], lo[:, k, t0:t0 + tw]
                    nc.tensor.matmul(out, wh, rh, start=first and k == 0, stop=False, skip_group_check=True)
                    nc.tensor.matmul(out, wh, rl, start=False, stop=False, skip_group_check=True)
                    mm = nc.tensor.matmul(out, wl, rh, start=False, stop=k == kt - 1, skip_group_check=True)
                return mm

            def whole(n, slot, kt, hi, lo, inputs=None):
                for c in range(3):
                    ready(n, c)
                    if inputs is not None:
                        inputs(c)
                    steps(slot, c, 0, kt, kt, hi, lo).then_inc(mm_done, 1)

            def transposed_x(c):
                for k in range(KT):
                    q = c * KT + k
                    if k == 0:
                        pe.wait_ge(x_norm, X_TILES[c][1])
                    if q >= 5:
                        pe.wait_ge(x_low, q - 4)
                    for i, t in enumerate(range(*X_TILES[c])):
                        mm = nc.tensor.transpose(bank[3 + q % 5][:, i * P:i * P + P], x_in[:, t, k * P:k * P + P],
                                                 ident[:])
                    mm.then_inc(x_tr, 1)

            def low_rank(c):
                pe.wait_ge(x_low, (c + 1) * KT)
                if c == 0:
                    pe.wait_ge(w_split, 2)
                steps(0, c, 0, KT, KT, act_hi, act_lo).then_inc(mm_done, 1)

            pe.wait_ge(ident_ready, 2)
            pe.wait_ge(primed, 1)
            transposed_x(0)
            transposed_x(1)
            low_rank(0)
            transposed_x(2)
            low_rank(1)
            low_rank(2)

            pe.wait_ge(const_dve, 2)

            def unit_steps(h, g, tau):
                u = 3 * h + g
                kz, qz, vz = (z[:, (3 * (g % 2)) + i, :] for i in range(3))
                if tau in (4, 9):
                    e = int(tau == 9)
                    pe.wait_ge(sq_ready, 2 * u + e + 2)
                    if e == 0:
                        if g == 0:
                            pe.wait_ge(head_done, h + 1)
                        pe.wait_ge(stt_read, u + 1)
                        pe.wait_ge(max_done, 10 * u + 1)
                    else:
                        pe.wait_ge(ln_done, 2 * u + 2)
                    for c, (t0, tw) in enumerate(CHUNKS):
                        mm = nc.tensor.matmul(bank[(3, 4, 7)[c]][:, 0:tw], ones[:], ar[:, e, t0:t0 + tw],
                                              start=True, stop=True)
                    mm.then_inc(ss_done, 1)
                if tau in (6, 7, 11):
                    i = (6, 7, 11).index(tau)
                    if i == 0:
                        pe.wait_ge(evac, slab_chunks(N_HEAD + 3 * g + 3) + h * (3 * SLOTS) + 1)
                        pe.wait_ge(prt_read, 10 * u + 1)
                    elif i == 1:
                        pe.wait_ge(o_read, 10 * u + 1)
                    else:
                        pe.wait_ge(vn_ready, 3 * u + 2)
                    for m in range(4 * i, min(4 * i + 4, BLK)):
                        for c0, c1 in value_tile(g, m):
                            mm = nc.tensor.transpose(bank[6 if i == 1 else 5][0:c1 - c0, (m % 4) * P:(m % 4 + 1) * P],
                                                     vz[:, c0:c1], ident[:])
                    mm.then_inc(vt_done, 1)
                b, at_ = divmod(tau - 18, BSTEP)
                if at_ == 0 and 0 <= b < BLK:
                    if b == 0:
                        pe.wait_ge(qk_ready, 2 * u + 3)
                    if b >= 2:
                        pe.wait_ge(max_done, 10 * u + b)
                    kk = keys(kz, g, b)
                    w = window(g, b)
                    nk = P if w is None else w[2] - w[1]
                    q0 = block_at(g, b)
                    nc.tensor.matmul(bank[3 + b % 2][:, 0:nk], qz[:, q0:q0 + P], kk,
                                     start=True, stop=True).then_inc(scores_done, 1)
                if at_ == 1 and 1 <= b <= BLK:
                    b -= 1
                    pe.wait_ge(exp_done, 10 * u + b + 2)
                    if b == 0:
                        pe.wait_ge(vn_ready, 3 * u + 4)
                    else:
                        pe.wait_ge(prt_read, 10 * u + b + 1)
                    for i, (m, p0, p1, c0) in enumerate(pieces(g, b)):
                        mm = nc.tensor.transpose(bank[5][:, i * P:i * P + P], pr[:, b % 2, c0:c0 + P], ident[:])
                    mm.then_inc(prt_done, 1)
                b, at_ = divmod(tau - 26, BSTEP)
                if at_ == 0 and 0 <= b < BLK:
                    pe.wait_ge(prt_read, 10 * u + b + 2)
                    if b >= 1:
                        pe.wait_ge(o_read, 10 * u + b + 1)
                    pc = pieces(g, b)
                    for i, (m, p0, p1, c0) in enumerate(pc):
                        mm = nc.tensor.matmul(bank[6][:, 0:P], ar[p0:p1, 2, m * P:m * P + P],
                                              prt[p0:p1, b % 2, i * P:i * P + P], start=i == 0, stop=i == len(pc) - 1)
                    mm.then_inc(pv_done, 1)
                if tau == T_STAT:
                    pe.wait_ge(exp_done, 10 * u + 11)
                    nc.tensor.transpose(bank[7][0:2 * BLK, 0:P], st[:, 0:2 * BLK], ident[:]).then_inc(stt_done, 1)

            def gla_steps(h, tick):
                if tick in T_LR:
                    d = T_LR.index(tick)
                    if d == 0:
                        pe.wait_ge(head_loaded, 64 * (h + 1))
                        pe.wait_ge(stt_read, 3 * h + 4)
                        pe.wait_ge(evac, 4)
                    else:
                        pe.wait_ge(y_read, 2 * h + 2)
                    for c, (t0, tw) in enumerate(CHUNKS):
                        mm = nc.tensor.matmul(bank[(3, 4, 7)[c]][:, 0:tw], wa2[32 * d:32 * d + RANK, :],
                                              lowrank[32 * d:32 * d + RANK, t0:t0 + tw], start=True, stop=True)
                    mm.then_inc(lr_done, 1)
                i, at_ = divmod(tick - T_VT, 4)
                if at_ == 0 and 0 <= i < NT // 2:
                    if i == 0:
                        pe.wait_ge(evac, slab_chunks(N_HEAD + 13) + h * (3 * SLOTS) + 1)
                        pe.wait_ge(o_read, 30 * h + 31)
                    if i >= 2:
                        pe.wait_ge(gvn_ready, 5 * h + i)
                    for q in range(4):
                        src = z[:, 0 if q % 2 else 5, :]
                        tile = 2 * i + q // 2
                        mm = nc.tensor.transpose(bank[5 + i % 2][:, q * P:q * P + P], src[:, tile * P:tile * P + P],
                                                 ident[:])
                    mm.then_inc(gvt_done, 1)

                def prelude(j):
                    if j == 0:
                        pe.wait_ge(prep_d, 8 * h + 9)
                    else:
                        pe.wait_ge(a_ready, 10 * h + j + 1)
                        pe.wait_ge(kdn_ready, 10 * h + j + 1)
                    fw, bw = slice(j * P, j * P + P), slice((NT - 1 - j) * P, (NT - j) * P)
                    nc.tensor.matmul(bank[3][:, 0:P], ar[:, 1, fw], ar[:, 0, fw], start=True, stop=True,
                                     skip_group_check=True)
                    nc.tensor.matmul(bank[3][:, P:2 * P], ar[:, 4, fw], ar[:, 3, fw], start=True, stop=True,
                                     skip_group_check=True)
                    nc.tensor.transpose(bank[3][:, 2 * P:3 * P], ar[:, 2, fw], ident[:])
                    nc.tensor.transpose(bank[3][:, 3 * P:4 * P], ar[:, 5, bw], ident[:]).then_inc(pre_done, 1)

                if tick == T_GLA - 4:
                    prelude(0)
                j, at_ = divmod(tick - T_GLA, GSTEP)
                if not 0 <= j < NT:
                    return
                jb = NT - 1 - j
                if at_ == 0:
                    pe.wait_ge(kdn_ready, 10 * h + j + 2)
                    if j == 0:
                        pe.wait_ge(gvn_ready, 5 * h + 6)
                        pe.wait_ge(y_read, 2 * h + 3)
                    else:
                        pe.wait_ge(s_ready, 40 * h + 4 * j + 1)
                    for d, (tile, order) in enumerate(((j, (0, 1)), (jb, (1, 0)))):
                        for ch in order:
                            mm = nc.tensor.matmul(bank[4 + ch][:, d * DV:(d + 1) * DV],
                                                  kdn[64 * ch:64 * ch + 64, j % 2, d, :],
                                                  keyvals[64 * ch:64 * ch + 64, tile, :],
                                                  start=True, stop=True, skip_group_check=True)
                        mm.then_inc(u_done, 1)
                if at_ == 1:
                    pe.wait_ge(a_ready, 10 * h + j + 2)
                    if 1 <= j <= 5:
                        pe.wait_ge(go_copied, 10 * h + 2 * j + 1)
                    elif j > 5:
                        pe.wait_ge(go_added, 10 * h + 2 * (j - 5) + 1)
                    for v in range(2):
                        nc.tensor.matmul(bank[6][:, v * P:v * P + P], keyvals[:, j, v * P:v * P + P],
                                         amat[:, j % 2, :], start=v == 0, stop=False, skip_group_check=True)
                if at_ in (1, 5):
                    i = int(at_ == 5)
                    for d, tile in ((0, j), (1, jb)):
                        if i == 1:
                            pe.wait_ge(s_ready, 40 * h + 4 * j + d + 2)
                        c0 = 64 * (i if d == 0 else 1 - i)
                        for v in range(2):
                            mm = nc.tensor.matmul(bank[6 + d][:, v * P + c0:v * P + c0 + 64],
                                                  state[:, d, i, v * P:v * P + P],
                                                  ar[:, 3 * d, tile * P + c0:tile * P + c0 + 64],
                                                  start=d == 1 and i == 0 and v == 0, stop=i == 1 and v == 1,
                                                  skip_group_check=True)
                        mm.then_inc(o_done if i else i0_done, 1)
                if at_ == 3 and j + 1 < NT:
                    prelude(j + 1)

            with pe.Fori(0, H) as h:
                for tick in range(24 * SLOTS):
                    t, c, k = tick // 24, tick % 24 // 8, tick % 8
                    if k == 0:
                        if c == 0:
                            pe.wait_ge(w_split, N_HEAD + t + 1 + h * SLOTS + 1)
                        pe.wait_ge(evac, slab_chunks(N_HEAD + t - 1) + c + 1 + h * (3 * SLOTS) + 1)
                    mm = steps((N_HEAD + t) % 2, c, k, k + 1, KT, act_hi, act_lo)
                    if k == 7:
                        mm.then_inc(mm_done, 1)
                    for g in range(3):
                        unit_steps(h, g, tick - 24 * (3 + 3 * g))
                    gla_steps(h, tick)
                pe.wait_ge(osq_ready, 2 * h + 3)
                pe.wait_ge(s_ready, 40 * h + 41)
                for c, (t0, tw) in enumerate(CHUNKS):
                    for v in range(2):
                        mm = nc.tensor.matmul(bank[3 + c][:, 0:tw], ones[:], ar[:, 10 + v, t0:t0 + tw],
                                              start=v == 0, stop=v == 1)
                    mm.then_inc(oss_done, 1)
            for j in range(REST):
                whole(N_REST + j, (N_REST + j) % 2, KT, act_hi, act_lo)

            with pe.Fori(0, KT) as j:
                n = N_C1 + 2 * j
                whole(n, N_C1 % 2, KT, act_hi, act_lo, lambda c: pe.wait_ge(c_low, 8 * c + 9))
                whole(n + 1, (N_C1 + 1) % 2, 4, ob_hi, ob_lo, lambda c: pe.wait_ge(c_low, 24 + 5))

            def column_sums(row, first, last):
                for c, (t0, tw) in enumerate(CHUNKS):
                    mm = nc.tensor.matmul(bank[3 + c][:, 0:tw], ones[:], work[:, row, t0:t0 + tw],
                                          start=first, stop=last, skip_group_check=True)
                return mm

            with pe.Fori(0, KT // 2) as i:
                for e in range(2):
                    n = N_C2 + e + 2 * i
                    xt = work[:, 16 + e, :].rearrange("p (n d) -> p n d", d=P)
                    for c, (t0, tw) in enumerate(CHUNKS):
                        ready(n, c)
                        pe.wait_ge(m_low, 8 * c + 9)
                        if c == 0:
                            pe.wait_ge(xn_loaded[e], 32 * i + 32)
                        for q in range(tw // P):
                            nc.tensor.matmul(bank[c][:, q * P:q * P + P], xt[:, t0 // P + q, :], ident[:],
                                             start=q == 0, stop=False, skip_group_check=True)
                        steps((N_C2 + e) % 2, c, 0, KT, KT, act_hi, act_lo, first=False).then_inc(mm_done, 1)
            pe.wait_ge(head_done, H + 1)
            pe.wait_ge(x1_acc, KT + 2)
            column_sums(8, True, True).then_inc(x1_ss, 1)

            with pe.Fori(0, ROUNDS) as i:
                for e in range(2):
                    whole(N_D + e + 4 * i, (N_D + e) % 2, KT, act_hi, act_lo, lambda c: pe.wait_ge(n_low, 8 * c + 9))
                for e in range(2):
                    n = N_D + 2 + e + 4 * i
                    pe.wait_ge(w_split, n + 2)
                    for c, (t0, tw) in enumerate(CHUNKS):
                        pe.wait_ge(u_low, 6 * i + 3 + c + 2)
                        for jt in range(4):
                            if jt < 3:
                                pe.wait_ge(w2_read, 18 * i + 9 * e + 3 * c + jt + 2)
                            else:
                                pe.wait_ge(evac, slab_chunks(n) + c + 1)
                            mm = steps((N_D + e) % 2, c, 0, 2, 2, u_hi, u_lo, out=bank[3 + jt][:, 0:tw],
                                       column=lambda k: 4 * k + jt)
                            mm.then_inc(mm_done if jt == 3 else w2_done, 1)

            def squares_and_p():
                pe.wait_ge(w2_read, 18 * ROUNDS + 4)
                for i in range(KT // 2):
                    pe.wait_ge(x1_acc, KT + 3 + i)
                    column_sums(14 + 2 * (i % 2), i == 0, i == KT // 2 - 1).then_inc(x1_ss, 1)
                pe.wait_ge(p_loaded, 64)
                pe.wait_ge(evac, slab_chunks(N_E) + 1)
                for i in range(5):
                    if i >= 2:
                        pe.wait_ge(p_low, i)
                    for q in range(4):
                        e, m = divmod(4 * i + q, NT)
                        mm = nc.tensor.transpose(bank[6 + i % 2][:, q * P:q * P + P],
                                                 work[:, 12 + e, m * P:m * P + P], ident[:])
                    mm.then_inc(p_tr, 1)

            def transposed_y(j):
                for c, (t0, tw) in enumerate(CHUNKS):
                    pe.wait_ge(y_ready, 3 * j + c + 2)
                    for q in range(tw // P):
                        mm = nc.tensor.transpose(bank[5 + c][:, q * P:q * P + P],
                                                 work[:, 17, t0 + q * P:t0 + q * P + P], ident[:])
                    mm.then_inc(yt_done, 1)

            def gate_tile(j, first):
                n = N_E + 2 * j
                for c in range(3):
                    ready(n, c)
                    pe.wait_ge(n_low, 24 + 8 * c + 9)
                    steps(N_E % 2, c, 0, KT, KT, act_hi, act_lo).then_inc(mm_done, 1)
                    if c == 0 and not first:
                        pe.wait_ge(yt_read, 3 * j - 2)
                        transposed_y(j - 1)
                if first:
                    squares_and_p()
                whole(n + 1, (N_E + 1) % 2, 2, u_hi, u_lo, lambda c: pe.wait_ge(p_low, 6))

            gate_tile(0, True)
            pe.wait_ge(n_ln, 4)
            with pe.Fori(1, KT) as j:
                gate_tile(j, False)
            pe.wait_ge(yt_read, 3 * KT - 2)
            transposed_y(KT - 1)

        @block.scalar
        def _(act):
            A = nc.scalar.activation
            own = Chain()

            def split_high(n, slot, width=1024):
                act.wait_ge(w_loaded, 16 * n + 32)
                act.wait_ge(mm_done, slab_chunks(n - 1) + 1)
                A(w_hi[:, slot, 0:width], w_raw[:, 0:width], ACT.Copy).then_inc(w_high, 1)

            def chunk_done(n, c):
                act.wait_ge(mm_done, slab_chunks(n) + c + 2)

            for dst, name in ((g_mix, "norm_mix_g"), (g_mlp, "norm_mlp_g"), (g_ple, "norm_ple_g"), (g_gla, "gla_norm_g")):
                act.dma_start(dst[:], a[name].rearrange("(k p) -> p k", p=P)).then_inc(const_dma, 16)
            for dst, name in ((g_q, "attn_qnorm_g"), (g_k, "attn_knorm_g")):
                act.dma_start(dst[:], a[name].rearrange("g p -> p g")).then_inc(const_dma, 16)
            act.wait_ge(w_zero, 1)
            lr = w_raw[:].rearrange("p (k n) -> p k n", n=P)
            act.dma_start(lr[:, :, 0:RANK], w_in[:, :, C_LR:C_LR + RANK]).then_inc(w_loaded, 16)
            act.dma_start(lr[:, :, 32:32 + RANK], w_in[:, :, C_LR + RANK:C_LR + 2 * RANK]).then_inc(w_loaded, 16)

            def squares(t):
                act.wait_ge(x_loaded[t], 16)
                if t:
                    act.wait_ge(x_sumsq, t)
                A(x_sq[:], x_in[:, t, :], ACT.Square, accum_out=ssx[:, t:t + 1]).then_inc(x_sumsq, 1)

            def x_highs(c):
                t0, tw = CHUNKS[c]
                for k in range(KT):
                    q = c * KT + k
                    act.wait_ge(x_tr, q + 1)
                    A(act_hi[:, k, t0:t0 + tw], bank[3 + q % 5][:, 0:tw], ACT.Copy, scale=g_mix[:, k:k + 1]
                      ).then_inc(x_high, 1)

            for t in range(4):
                squares(t)
            act.wait_ge(primed, 1)
            act.wait_ge(w_loaded, 32)
            A(w_hi[:, 0, :], w_raw[:], ACT.Copy).then_inc(w_high, 1)
            for t in range(4, NT):
                squares(t)
            act.wait_ge(const_dma, 96)
            x_highs(0)
            act.wait_ge(w_loaded, 48)
            A(w_hi[:, 1, :], w_raw[:], ACT.Copy).then_inc(w_high, 1)
            x_highs(1)
            x_highs(2)
            for c, (t0, tw) in enumerate(CHUNKS):
                act.wait_ge(mm_done, c + 2)
                A(lowrank[:, t0:t0 + tw], bank[c][0:48, 0:tw], ACT.Copy).then_inc(evac, 1)

            act.wait_ge(const_pool, 2)
            act.wait_ge(const_dve, 2)

            def unit_steps(h, g, tau):
                u = 3 * h + g
                kz, qz = (z[:, 3 * (g % 2) + i, :] for i in range(2))
                if tau == 2:
                    if g == 0:
                        act.wait_ge(head_done, h + 1)
                    act.wait_ge(evac, slab_chunks(N_HEAD + 3 * g + 3) + h * (3 * SLOTS) + 1)
                    act.wait_ge(qk_ready, 2 * u + 1)
                    A(ar[:, 0, :], kz, ACT.Square).then_inc(sq_ready, 1)
                    A(ar[:, 1, :], qz, ACT.Square).then_inc(sq_ready, 1)
                if tau in (8, 12):
                    e = int(tau == 12)
                    act.wait_ge(ss_done, 2 * u + e + 2)
                    for c, (t0, tw) in enumerate(CHUNKS):
                        ins = A(ar[:, e, t0:t0 + tw], bank[(3, 4, 7)[c]][:, 0:tw], ACT.Ln, bias=eps[:], scale=1.0 / P)
                    ins.then_inc(ln_done, 1)
                if tau == 13:
                    act.wait_ge(ln_done, 2 * u + 3)
                    for e in range(2):
                        A(ar[:, e, :], ar[:, e, :], ACT.Exp, scale=-0.5).then_inc(r_ready, 1)
                b, at_ = divmod(tau - 20, BSTEP)
                if at_ == 0 and 0 <= b < BLK:
                    act.wait_ge(max_done, 10 * u + b + 2)
                    w = window(g, b)
                    nk = P if w is None else w[2] - w[1]
                    A(pr[:, b % 2, 0:nk], pr[:, b % 2, 0:nk], ACT.Exp, bias=st[:, b:b + 1], scale=-1.0,
                      accum_out=st[:, BLK + b:BLK + b + 1]).then_inc(exp_done, 1)
                b, at_ = divmod(tau - 24, BSTEP)
                if at_ == 0 and 0 <= b < BLK:
                    act.wait_ge(prt_done, 10 * u + b + 2)
                    if b >= 2:
                        act.wait_ge(pv_done, 10 * u + b)
                    w_ = P * len(pieces(g, b))
                    A(prt[:, b % 2, 0:w_], bank[5][:, 0:w_], ACT.Copy).then_inc(prt_read, 1)

            def gla_steps(h, tick):
                if tick == T_CW + 1:
                    act.wait_ge(cexp_in, h + 2)
                    A(cw[:, 0:3, :], cw[:, 0:3, :], ACT.Exp).then_inc(cexp_out, 1)
                if tick - 2 in T_LR:
                    d = T_LR.index(tick - 2)
                    act.wait_ge(lr_done, 2 * h + d + 2)
                    if d == 1:
                        act.wait_ge(prep_a, 6 * h + 4)
                        act.wait_ge(prep_d, 8 * h + 5)
                    for c, (t0, tw) in enumerate(CHUNKS):
                        ins = A(ar[:, 10, t0:t0 + tw], bank[(3, 4, 7)[c]][:, 0:tw], ACT.Identity, bias=ba[:, d:d + 1])
                    ins.then_inc(y_read, 1)
                if tick - 4 in T_LR:
                    d = T_LR.index(tick - 4)
                    act.wait_ge(prep_d, 8 * h + 4 * d + 2)
                    A(ar[:, 11, :], ar[:, 11, :], ACT.Exp).then_inc(act_own, 1)
                    act.wait_ge(act_own, own.value())
                    A(ar[:, 11, :], ar[:, 11, :], ACT.Ln, bias=ones[:, 0:1]).then_inc(prep_a, 1)
                if tick in T_DECAY:
                    d = T_DECAY.index(tick)
                    act.wait_ge(prep_d, 8 * h + 4 * d + 3)
                    if d == 0:
                        act.wait_ge(pv_done, 30 * h + 31)
                        act.wait_ge(qk_ready, 6 * h + 7)
                    else:
                        act.wait_ge(ob_stored, 16 * h + 16)
                        act.wait_ge(ob_ready, h + 2)
                    r = 3 * d
                    A(ar[:, r, :], ar[:, 11, :], ACT.Exp, scale=1.0 / 16).then_inc(act_own, 1)
                    act.wait_ge(act_own, own.value())
                    A(ar[:, r + 1, :], ar[:, 11, :], ACT.Exp, scale=-1.0 / 16).then_inc(prep_a, 1)
                    last = ar[:, 11, :].rearrange("p (c l) -> p c l", l=64)[:, :, 63 * (1 - d)]
                    A(ebl[:, d, :], last, ACT.Exp, scale=1.0 / 16).then_inc(act_own, 1)
                    act.wait_ge(act_own, own.value())
                    act.wait_ge(prep_d, 8 * h + 4 * d + 4)
                    A(ar[:, r + 2, :], ar[:, 10, :], ACT.Exp, scale=1.0 / 16).then_inc(prep_a, 1)
                i, at_ = divmod(tick - T_VT - 4, 4)
                if at_ == 0 and 0 <= i < NT // 2:
                    if i == 0:
                        act.wait_ge(ob_ready, h + 2)
                    act.wait_ge(gvt_done, 5 * h + i + 2)
                    A(keyvals[:, 2 * i:2 * i + 2, :], bank[5 + i % 2][:].rearrange("p (n v) -> p n v", v=DV), ACT.Copy
                      ).then_inc(gvn_ready, 1)

                def decayed(j):
                    act.wait_ge(pre_done, 10 * h + j + 2)
                    if j >= 2:
                        act.wait_ge(u_done, 20 * h + 2 * j - 1)
                    A(kdn[:, j % 2, :, :], bank[3][:, 2 * P:4 * P].rearrange("p (d s) -> p d s", d=2), ACT.Copy
                      ).then_inc(kdn_ready, 1)

                if tick == T_GLA - 3:
                    decayed(0)
                j, at_ = divmod(tick - T_GLA, GSTEP)
                if 0 <= j < NT and at_ == 3 and j + 1 < NT:
                    decayed(j + 1)
                j, at_ = divmod(tick - T_GLA - 6, GSTEP)
                if 0 <= j < 5 and at_ == 0:
                    if j == 0:
                        act.wait_ge(prep_d, 8 * h + 9)
                    for d, tile in ((0, j), (1, NT - 1 - j)):
                        act.wait_ge(o_done, 20 * h + 2 * j + d + 2)
                        A(o_gla[:, :, tile * P:tile * P + P], bank[6 + d][:, 0:DV].rearrange("p (v t) -> p v t", v=2),
                          ACT.Copy).then_inc(go_copied, 1)

            start = own.base + own.n
            with act.Fori(0, H) as h:
                own.enter(h, 10)
                for tick in range(24 * SLOTS + 1):
                    t, r = divmod(tick, 24)
                    if tick % 8 == 0 and tick:
                        tt, c = divmod(tick // 8 - 1, 3)
                        if c == 0:
                            if tt < 3:
                                act.wait_ge(head_done, h + 1)
                            elif tt < 6:
                                act.wait_ge(gate_stored, 48 * h + 16)
                            elif tt < 15:
                                act.wait_ge(scores_done, 30 * h + 10 * (tt // 3 - 1) + 1)
                            elif tt == 15:
                                act.wait_ge(prep_d, 8 * h + 9)
                            elif tt == 17:
                                act.wait_ge(gvt_done, 5 * h + 6)
                        n = N_HEAD + tt + h * SLOTS
                        t0, tw = CHUNKS[c]
                        chunk_done(n, c)
                        dst, src = work[:, Z_OF[tt], t0:t0 + tw], bank[c][:, 0:tw]
                        if 3 <= tt < 9:
                            dst = by_residue(work[:, Z_OF[tt], :], tt // 3, c)
                            src = src.rearrange("p (l r) -> p r l", r=dst.shape[1])
                        A(dst, src, ACT.Copy, scale=DK ** -0.5 if tt == 9 else 1.0).then_inc(evac, 1)
                    if tick == 24 * SLOTS:
                        break
                    if r == 1:
                        split_high(N_HEAD + t + 1 + h * SLOTS, (N_HEAD + t + 1) % 2)
                    for g in range(3):
                        unit_steps(h, g, tick - 24 * (3 + 3 * g))
                    gla_steps(h, tick)
                act.wait_ge(go_added, 10 * h + 11)
                for v in range(2):
                    A(ar[:, 10 + v, :], o_gla[:, v, :], ACT.Square).then_inc(osq_ready, 1)
                act.wait_ge(oss_done, 3 * h + 4)
                for c, (t0, tw) in enumerate(CHUNKS):
                    A(ar[:, 10, t0:t0 + tw], bank[3 + c][:, 0:tw], ACT.Ln, bias=eps[:], scale=1.0 / DV).then_inc(act_own, 1)
                    act.wait_ge(act_own, own.value())
                A(ar[:, 10, :], ar[:, 10, :], ACT.Exp, scale=-0.5).then_inc(act_own, 1)
                act.wait_ge(act_own, own.value())
                A(ar[:, 11, :], z[:, 1, :], ACT.Sigmoid).then_inc(gate_ready, 1)
                A(ar[:, 0, :], z[:, 2, :], ACT.Sigmoid).then_inc(gate_ready, 1)
            own.leave(H, start)

            for j in range(REST):
                split_high(N_REST + j + 1, (N_REST + j + 1) % 2)
                if j == 0:
                    act.wait_ge(head_done, H + 1)
                for c, (t0, tw) in enumerate(CHUNKS):
                    if c == 0 and j >= 2:
                        act.wait_ge(rest_stored[j % 2], 16 * (j // 2))
                    chunk_done(N_REST + j, c)
                    A(work[:, 16 + j % 2, t0:t0 + tw], bank[c][:, 0:tw], ACT.Copy).then_inc(evac, 1)
                    if j == REST - 1:
                        if c == 0:
                            act.wait_ge(oa_loaded, 16 * KT)
                        for k in range(KT):
                            A(act_hi[:, k, t0:t0 + tw], merged[:, k, t0:t0 + tw], ACT.Copy).then_inc(c_high, 1)
            act.wait_ge(ob_loaded, 64)
            for k in range(4):
                A(ob_hi[:, k, :], work[:, 4 + k, :], ACT.Copy).then_inc(c_high, 1)

            with act.Fori(0, KT) as j:
                n = N_C1 + 2 * j
                split_high(n + 1, (N_C1 + 1) % 2, 512)
                for e in range(2):
                    act.wait_ge(g_loaded, 32 * j + 32)
                    A(work[:, 16 + e, :], work[:, 16 + e, :], ACT.Sigmoid).then_inc(g_sig, 1)
                split_high(n + 2, N_C1 % 2)
            for c, (t0, tw) in enumerate(CHUNKS):
                chunk_done(N_C2 - 2, c)
                for k in range(KT):
                    act.wait_ge(m_done, 3 * k + c + 2)
                    A(act_hi[:, k, t0:t0 + tw], merged[:, k, t0:t0 + tw], ACT.Copy).then_inc(m_high, 1)

            act.wait_ge(m_low, 3 * KT + 1)
            with act.Fori(0, KT // 2) as i:
                for e in range(2):
                    n = N_C2 + e + 2 * i
                    split_high(n + 1, (N_C2 + e + 1) % 2)
                    row = work[:, bass.ds(2 * i + e, 1), :].rearrange("p o t -> p (o t)")
                    for c, (t0, tw) in enumerate(CHUNKS):
                        act.wait_ge(mm_done, slab_chunks(n) + c + 2)
                        act.sem_inc(act_passed, 1)
                        A(row[:, t0:t0 + tw], bank[c][:, 0:tw], ACT.Copy).then_inc(evac, 1)
                    act.wait_ge(evac, slab_chunks(n + 1) + 1)
                    act.wait_ge(x1_acc, 2 * i + e + 1)
                    act.sem_inc(act_passed, 1)
                    A(work[:, 12 + e, :], row, ACT.Square).then_inc(x1_sq, 1)

            def norm_rows(gain):
                for c, (t0, tw) in enumerate(CHUNKS):
                    for k in range(KT):
                        A(act_hi[:, k, t0:t0 + tw], xres[:, k, t0:t0 + tw], ACT.Copy, scale=gain[:, k:k + 1]
                          ).then_inc(n_high, 1)

            norm_rows(g_mlp)
            act.wait_ge(x1_ss, 2)
            for c, (t0, tw) in enumerate(CHUNKS):
                A(r_bc[:, t0:t0 + tw], bank[3 + c][:, 0:tw], ACT.Ln, bias=eps[:], scale=1.0 / D).then_inc(w2_read, 1)
            act.wait_ge(w2_read, 4)
            A(r_bc[:], r_bc[:], ACT.Exp, scale=-0.5).then_inc(n_r, 1)

            with act.Fori(0, ROUNDS) as i:
                for e in range(4):
                    n = N_D + e + 4 * i
                    split_high(n + 1, (N_D + e + 1) % 2)
                    if e >= 2:
                        continue
                    for c, (t0, tw) in enumerate(CHUNKS):
                        q = 6 * i + 3 * e + c
                        buf = utmp[:, (3 * e + c) % 2, 0:tw]
                        act.wait_ge(evac, slab_chunks(n) + c + 2)
                        A(buf, buf, ACT.Square).then_inc(u_sq, 1)
                        act.wait_ge(u_sq, q + 2)
                        A(u_hi[:, e, t0:t0 + tw], buf, ACT.Copy).then_inc(u_high, 1)

            chunk_done(N_E - 1, 2)
            act.wait_ge(evac, slab_chunks(N_E) + 1)
            act.wait_ge(w2_read, 18 * ROUNDS + 4)
            norm_rows(g_ple)
            for k in range(KT):
                if k >= 4:
                    act.wait_ge(x1_ss, k // 2 + 1)
                A(work[:, 14 + k % 4, :], xres[:, k, :], ACT.Square).then_inc(x1_sq, 1)
            act.wait_ge(x1_ss, KT // 2 + 2)
            act.wait_ge(n_r, 2)
            for c, (t0, tw) in enumerate(CHUNKS):
                A(r_bc[:, t0:t0 + tw], bank[3 + c][:, 0:tw], ACT.Ln, bias=eps[:], scale=1.0 / D).then_inc(n_ln, 1)
            act.wait_ge(n_ln, 4)
            A(r_bc[:], r_bc[:], ACT.Exp, scale=-0.5).then_inc(n_r, 1)
            for i in range(5):
                act.wait_ge(p_tr, i + 2)
                A(u_hi[:].rearrange("p a t -> p (a t)")[:, 512 * i:512 * i + 512], bank[6 + i % 2][:], ACT.Copy
                  ).then_inc(p_high, 1)

            def y_out(j):
                act.wait_ge(y_stored, 32 * j + 16)
                for c, (t0, tw) in enumerate(CHUNKS):
                    act.wait_ge(yt_done, 3 * j + c + 2)
                    A(work[:, 16, t0:t0 + tw], bank[5 + c][:, 0:tw], ACT.Copy).then_inc(yt_read, 1)

            def gate_tile(j, first, last):
                n = N_E + 2 * j
                split_high(n + 1, (N_E + 1) % 2, 256)
                if not first:
                    y_out(j - 1)
                for c, (t0, tw) in enumerate(CHUNKS):
                    act.wait_ge(evac, slab_chunks(n) + c + 2)
                    A(work[:, 17, t0:t0 + tw], work[:, 17, t0:t0 + tw], ACT.Sigmoid).then_inc(pg_sig, 1)
                if not last:
                    split_high(n + 2, N_E % 2)

            gate_tile(0, True, False)
            with act.Fori(1, KT - 1) as j:
                gate_tile(j, False, False)
            gate_tile(KT - 1, False, True)
            y_out(KT - 1)

        @block.vector
        def _(dve):
            v_ = nc.vector
            own = Chain()

            def split_low(n, slot, width=1024):
                dve.wait_ge(w_high, n + 2)
                v_.tensor_tensor(w_lo[:, slot, 0:width], w_raw[:, 0:width], w_hi[:, slot, 0:width].bitcast(F32),
                                 ALU.subtract).then_inc(w_split, 1)

            def chunk_done(n, c):
                dve.wait_ge(mm_done, slab_chunks(n) + c + 2)

            v_.memset(w_raw[:], 0.0).then_inc(w_zero, 1)
            dve.wait_ge(primed, 1)
            v_.memset(ones[:], 1.0).then_inc(dve_own, 1)
            dve.wait_ge(dve_own, own.value())
            dve.wait_ge(const_dma, 96)
            v_.tensor_scalar(g_k[:], g_k[:], -(P ** -0.5), None, ALU.mult).then_inc(const_dve, 1)

            def normed_x(c):
                dve.wait_ge(x_r, c + 1)
                for t in range(*X_TILES[c]):
                    v_.tensor_scalar(x_in[:, t, :], x_in[:, t, :], rx[:, t:t + 1], None, ALU.mult).then_inc(x_norm, 1)

            def x_lows(c):
                t0, tw = CHUNKS[c]
                for k in range(KT):
                    q = c * KT + k
                    dve.wait_ge(x_high, q + 1)
                    v_.scalar_tensor_tensor(out=act_lo[:, k, t0:t0 + tw], in0=bank[3 + q % 5][:, 0:tw],
                                            scalar=g_mix[:, k:k + 1], in1=act_hi[:, k, t0:t0 + tw].bitcast(F32),
                                            op0=ALU.mult, op1=ALU.subtract).then_inc(x_low, 1)

            normed_x(0)
            split_low(0, 0)
            normed_x(1)
            x_lows(0)
            normed_x(2)
            split_low(1, 1)
            x_lows(1)
            x_lows(2)

            dve.wait_ge(const_pool, 2)

            def unit_steps(h, g, tau):
                u = 3 * h + g
                kz, qz = (z[:, 3 * (g % 2) + i, :] for i in range(2))
                if tau == 1:
                    dve.wait_ge(max_done, 10 * u + 1)
                    v_.tensor_scalar(bias_w[:], dist_w[:], slope[:, g:g + 1], None, ALU.mult).then_inc(dve_own, 1)
                    dve.wait_ge(dve_own, own.value())
                    if g:
                        v_.tensor_scalar(bias_b[:], dist_2[:], slope[:, g:g + 1], None, ALU.mult).then_inc(dve_own, 1)
                        dve.wait_ge(dve_own, own.value())
                if tau in (8, 9, 12):
                    i = (8, 9, 12).index(tau)
                    m0, m1 = 4 * i, min(4 * i + 4, BLK)
                    dve.wait_ge(vt_done, 3 * u + i + 2)
                    if i == 0 and g:
                        dve.wait_ge(pv_done, 10 * u + 1)
                    v_.tensor_copy(ar[:, 2, m0 * P:m1 * P], bank[6 if i == 1 else 5][:, 0:(m1 - m0) * P]
                                   ).then_inc(vn_ready, 1)
                if tau == 15:
                    for e, (zz, gain) in enumerate(((kz, g_k), (qz, g_q))):
                        dve.wait_ge(r_ready, 2 * u + e + 2)
                        v_.scalar_tensor_tensor(out=zz, in0=zz, scalar=gain[:, g:g + 1], in1=ar[:, e, :],
                                                op0=ALU.mult, op1=ALU.mult).then_inc(qk_ready, 1)
                b, at_ = divmod(tau - 19, BSTEP)
                if at_ == 0 and 0 <= b < BLK:
                    if g == 2 and b == 8:
                        dve.wait_ge(max_done, 10 * u + b + 1)
                        v_.tensor_scalar(bias_b[:], dist_8[:], slope[:, g:g + 1], None, ALU.mult).then_inc(dve_own, 1)
                        dve.wait_ge(dve_own, own.value())
                    dve.wait_ge(scores_done, 10 * u + b + 2)
                    if b == 0:
                        dve.wait_ge(stt_done, u + 1)
                        dve.wait_ge(prt_done, 10 * u + 1)
                    if b >= 2:
                        dve.wait_ge(prt_done, 10 * u + b)
                    w = window(g, b)
                    if w is None:
                        nk, bias = P, bias_b[:]
                    else:
                        nk = w[2] - w[1]
                        b0 = w[1] - (w[0] - 64)
                        bias = bias_w[:, b0:b0 + nk]
                    dve.sem_inc(dve_passed, 1)
                    v_.tensor_tensor_reduce(out=pr[:, b % 2, 0:nk], in0=bank[3 + b % 2][:, 0:nk], in1=bias, scale=1.0,
                                            scalar=3e38, op0=ALU.add, op1=ALU.min, accum_out=st[:, b:b + 1]
                                            ).then_inc(max_done, 1)
                b, at_ = divmod(tau - 28, BSTEP)
                if at_ == 0 and 0 <= b < BLK:
                    dve.wait_ge(pv_done, 10 * u + b + 2)
                    q = queries(ar[:, 3 + g, :], g, b)
                    v_.tensor_copy(q, like(bank[6][:, 0:P], q)).then_inc(o_read, 1)
                if tau == T_STAT + 2:
                    dve.wait_ge(stt_done, u + 2)
                    dve.wait_ge(stat_stored, 192 * h + 16 * (0, 2, 8)[g] + 16)
                    v_.tensor_copy(st_t[:], bank[7][0:2 * BLK, 0:P]).then_inc(stt_read, 1)

            def gla_steps(h, tick):
                if tick == T_CW:
                    dve.wait_ge(cst_loaded, 16 * h + 16)
                    dve.wait_ge(cw_stored, 16 * h + 16)
                    m = cw[:, 3, :]
                    v_.tensor_tensor(m, cst[:, 0, :], cst[:, 1, :], ALU.min).then_inc(dve_own, 1)
                    dve.wait_ge(dve_own, own.value())
                    v_.tensor_tensor(m, m, cst[:, 2, :], ALU.min).then_inc(dve_own, 1)
                    dve.wait_ge(dve_own, own.value())
                    v_.tensor_tensor(cw[:, 0:3, :], m.unsqueeze(1).broadcast_to([P, 3, NT]), cst[:, 0:3, :],
                                     ALU.subtract).then_inc(cexp_in, 1)
                if tick == T_CW + 3:
                    dve.wait_ge(cexp_out, h + 2)
                    m = cw[:, 3, :]
                    v_.tensor_tensor(cst[:, 3:6, :], cst[:, 3:6, :], cw[:, 0:3, :], ALU.mult).then_inc(dve_own, 1)
                    dve.wait_ge(dve_own, own.value())
                    v_.tensor_tensor(m, cst[:, 3, :], cst[:, 4, :], ALU.add).then_inc(dve_own, 1)
                    dve.wait_ge(dve_own, own.value())
                    v_.tensor_tensor(m, m, cst[:, 5, :], ALU.add).then_inc(dve_own, 1)
                    dve.wait_ge(dve_own, own.value())
                    v_.reciprocal(m, m).then_inc(dve_own, 1)
                    dve.wait_ge(dve_own, own.value())
                    v_.tensor_tensor(cw[:, 0:3, :], cw[:, 0:3, :], m.unsqueeze(1).broadcast_to([P, 3, NT]),
                                     ALU.mult).then_inc(cw_ready, 1)
                if tick == T_COMBINE:
                    dve.wait_ge(wb_loaded, 48 * h + 48)
                    for g in range(3):
                        v_.tensor_tensor(ar[:, 3 + g, :], ar[:, 3 + g, :], ar[:, WB[g], :], ALU.mult).then_inc(dve_own, 1)
                        dve.wait_ge(dve_own, own.value())
                    v_.tensor_tensor(ar[:, 3, :], ar[:, 3, :], ar[:, 4, :], ALU.add).then_inc(dve_own, 1)
                    dve.wait_ge(dve_own, own.value())
                    v_.tensor_tensor(ar[:, 3, :], ar[:, 3, :], ar[:, 5, :], ALU.add).then_inc(ob_ready, 1)
                if tick - 3 in T_LR:
                    d = T_LR.index(tick - 3)
                    dve.wait_ge(y_read, 2 * h + d + 2)
                    if d == 1:
                        dve.wait_ge(prep_a, 6 * h + 4)
                    v_.scalar_tensor_tensor(out=ar[:, 11, :], in0=ar[:, 10, :], scalar=-1.0, in1=ar[:, 10, :],
                                            op0=ALU.mult, op1=ALU.min).then_inc(prep_d, 1)
                if tick - 6 in T_LR:
                    d = T_LR.index(tick - 6)
                    way = slice(None, None, -1) if d else slice(None)
                    dve.wait_ge(prep_a, 6 * h + 3 * d + 2)
                    v_.scalar_tensor_tensor(out=ar[:, 10, :], in0=ar[:, 10, :], scalar=0.0, in1=ar[:, 11, :],
                                            op0=ALU.min, op1=ALU.subtract).then_inc(dve_own, 1)
                    dve.wait_ge(dve_own, own.value())
                    dve.wait_ge(carry_ready, 2 * h + d + 2)
                    v_.tensor_tensor_scan(ar[:, 11, way], ar[:, 8, way], ar[:, 10, way], 0.0, ALU.mult, ALU.add
                                          ).then_inc(prep_d, 1)
                    dve.wait_ge(prep_d, 8 * h + 4 * d + 3)
                    b = ar[:, 11, :].rearrange("p (c l) -> p c l", l=64)
                    e = 63 * (1 - d)
                    v_.tensor_tensor(ar[:, 10, :].rearrange("p (c l) -> p c l", l=64),
                                     b[:, :, e:e + 1].broadcast_to([P, T // 64, 64]), b, ALU.subtract).then_inc(prep_d, 1)
                if tick in T_QK:
                    d = T_QK.index(tick)
                    dve.wait_ge(prep_a, 6 * h + 3 * d + 3)
                    v_.tensor_tensor(ar[:, 3 * d, :], ar[:, 3 * d, :], z[:, 4, :], ALU.mult).then_inc(dve_own, 1)
                    dve.wait_ge(dve_own, own.value())
                    v_.tensor_tensor(ar[:, 3 * d + 1, :], ar[:, 3 * d + 1, :], z[:, 3, :], ALU.mult).then_inc(dve_own, 1)
                    dve.wait_ge(dve_own, own.value())
                    dve.wait_ge(prep_a, 6 * h + 3 * d + 4)
                    v_.tensor_tensor(ar[:, 3 * d + 2, :], ar[:, 3 * d + 2, :], z[:, 3, :], ALU.mult).then_inc(prep_d, 1)
                if tick == T_COMBINE + 3:
                    dve.wait_ge(prt_read, 30 * h + 31)
                    v_.memset(amat[:], 0.0).then_inc(dve_own, 1)
                    dve.wait_ge(dve_own, own.value())
                    v_.memset(state[:], 0.0).then_inc(dve_own, 1)
                    dve.wait_ge(dve_own, own.value())

                def masked(j):
                    dve.wait_ge(kdn_ready, 10 * h + j + 2)
                    dve.sem_inc(dve_passed, 1)
                    v_.copy_predicated(amat[:, j % 2, :], mask_f[:], bank[3][:, 0:P]).then_inc(dve_own, 1)
                    dve.wait_ge(dve_own, own.value())
                    dve.sem_inc(dve_passed, 1)
                    v_.copy_predicated(amat[:, j % 2, :], mask_b[:], bank[3][:, P:2 * P]).then_inc(a_ready, 1)

                def update(j, i, d):
                    tile = j if d == 0 else NT - 1 - j
                    half_ = i if d == 0 else 1 - i
                    ch = 2 * tile + half_
                    if i == 1 and (d, j) in ((0, TS // P - 1), (1, TP // P - 1)):
                        ins = v_.memset(state[:, d, 0, :], 0.0)
                    else:
                        ins = v_.scalar_tensor_tensor(out=state[:, d, 1 - i, :], in0=state[:, d, i, :],
                                                      scalar=ebl[:, d, ch:ch + 1], in1=bank[4 + half_][:, d * DV:(d + 1) * DV],
                                                      op0=ALU.mult, op1=ALU.add)
                    ins.then_inc(s_ready, 1)

                if tick == T_GLA - 2:
                    masked(0)
                j, at_ = divmod(tick - T_GLA, GSTEP)
                if 0 <= j < NT:
                    if at_ == 1:
                        dve.wait_ge(u_done, 20 * h + 2 * j + 3)
                        for d in range(2):
                            if j:
                                dve.wait_ge(o_done, 20 * h + 2 * j + 1)
                                dve.wait_ge(s_ready, 40 * h + 4 * j + 1)
                            update(j, 0, d)
                    if at_ == 4:
                        for d in range(2):
                            dve.wait_ge(i0_done, 20 * h + 2 * j + d + 2)
                            dve.wait_ge(s_ready, 40 * h + 4 * j + d + 2)
                            update(j, 1, d)
                        if j + 1 < NT:
                            masked(j + 1)
                j, at_ = divmod(tick - T_GLA - 6, GSTEP)
                if 5 <= j < NT and at_ == 0:
                    for d, tile in ((0, j), (1, NT - 1 - j)):
                        dve.wait_ge(o_done, 20 * h + 2 * j + d + 2)
                        if j == 5:
                            dve.wait_ge(go_copied, 10 * h + 11)
                        o = o_gla[:, :, tile * P:tile * P + P]
                        v_.tensor_tensor(o, bank[6 + d][:, 0:DV].rearrange("p (v t) -> p v t", v=2), o, ALU.add
                                         ).then_inc(go_added, 1)

            start = own.base + own.n
            with dve.Fori(0, H) as h:
                own.enter(h, 40)
                dve.wait_ge(head_done, h + 1)
                v_.tensor_copy(slope[:], slopes[:, bass.ds(3 * h, 3)]).then_inc(dve_own, 1)
                dve.wait_ge(dve_own, own.value())
                for tick in range(24 * SLOTS):
                    t, r = divmod(tick, 24)
                    if r == 2:
                        split_low(N_HEAD + t + 1 + h * SLOTS, (N_HEAD + t + 1) % 2)
                    for g in range(3):
                        unit_steps(h, g, tick - 24 * (3 + 3 * g))
                    gla_steps(h, tick)
                for v, row in enumerate((11, 0)):
                    dve.wait_ge(gate_ready, 2 * h + v + 2)
                    v_.tensor_tensor(ar[:, row, :], ar[:, row, :], z[:, 1 + v, :], ALU.mult).then_inc(dve_own, 1)
                    dve.wait_ge(dve_own, own.value())
                    v_.tensor_tensor(ar[:, row, :], ar[:, row, :], ar[:, 10, :], ALU.mult).then_inc(dve_own, 1)
                    dve.wait_ge(dve_own, own.value())
                    last = v_.scalar_tensor_tensor(out=o_gla[:, v, :], in0=o_gla[:, v, :], scalar=g_gla[:, v:v + 1],
                                                   in1=ar[:, row, :], op0=ALU.mult, op1=ALU.mult)
                    if v == 0:
                        last.then_inc(dve_own, 1)
                        dve.wait_ge(dve_own, own.value())
                last.then_inc(head_done, 1)
            own.leave(H, start)

            for j in range(REST):
                split_low(N_REST + j + 1, (N_REST + j + 1) % 2)
            q = 0
            for c, (t0, tw) in enumerate(CHUNKS):
                for k in range(KT):
                    q += 1
                    dve.wait_ge(c_high, q + 1)
                    v_.tensor_tensor(act_lo[:, k, t0:t0 + tw], merged[:, k, t0:t0 + tw],
                                     act_hi[:, k, t0:t0 + tw].bitcast(F32), ALU.subtract).then_inc(c_low, 1)
            for k in range(4):
                q += 1
                dve.wait_ge(c_high, q + 1)
                v_.tensor_tensor(ob_lo[:, k, :], work[:, 4 + k, :], ob_hi[:, k, :].bitcast(F32), ALU.subtract
                                 ).then_inc(c_low, 1)

            def merged_low(c, k):
                t0, tw = CHUNKS[c]
                dve.wait_ge(m_high, c * KT + k + 2)
                v_.tensor_tensor(act_lo[:, k, t0:t0 + tw], merged[:, k, t0:t0 + tw],
                                 act_hi[:, k, t0:t0 + tw].bitcast(F32), ALU.subtract).then_inc(m_low, 1)

            def merge_tile(j, last):
                n = N_C1 + 2 * j
                split_low(n + 1, (N_C1 + 1) % 2, 512)
                for e in range(2):
                    if e == 1:
                        split_low(n + 2, N_C1 % 2)
                    dve.wait_ge(g_sig, 2 * j + e + 2)
                    for c, (t0, tw) in enumerate(CHUNKS):
                        if last and e == 1:
                            for k in range(KT - 1):
                                merged_low(c, k)
                        gate = work[:, 16 + e, t0:t0 + tw]
                        chunk_done(n + e, c)
                        v_.tensor_tensor(gate, bank[c][:, 0:tw], gate, ALU.mult).then_inc(evac, 1)
                        if e == 1:
                            dve.wait_ge(evac, slab_chunks(n + 1) + c + 2)
                            both = merged[:, bass.ds(j, 1), t0:t0 + tw].rearrange("p o t -> p (o t)")
                            v_.tensor_tensor(both, work[:, 16, t0:t0 + tw], gate, ALU.add).then_inc(m_done, 1)
                            if last:
                                merged_low(c, KT - 1)

            with dve.Fori(0, KT - 1) as j:
                merge_tile(j, False)
            merge_tile(KT - 1, True)

            dve.wait_ge(m_low, 3 * KT + 1)
            v_.memset(work[:, 8, :], 0.0).then_inc(x1_acc, 1)
            with dve.Fori(0, KT // 2) as i:
                for e in range(2):
                    split_low(N_C2 + e + 1 + 2 * i, (N_C2 + e + 1) % 2)
                    dve.wait_ge(x1_acc, 2 * i + e + 2)
                    dve.wait_ge(x1_sq, 2 * i + e + 2)
                    v_.tensor_tensor(work[:, 8, :], work[:, 8, :], work[:, 12 + e, :], ALU.add).then_inc(x1_acc, 1)

            def norm_rows(gain, before):
                for c, (t0, tw) in enumerate(CHUNKS):
                    for k in range(KT):
                        dve.wait_ge(n_high, before + c * KT + k + 2)
                        v_.scalar_tensor_tensor(out=act_lo[:, k, t0:t0 + tw], in0=xres[:, k, t0:t0 + tw],
                                                scalar=gain[:, k:k + 1], in1=act_hi[:, k, t0:t0 + tw].bitcast(F32),
                                                op0=ALU.mult, op1=ALU.subtract).then_inc(n_low, 1)

            norm_rows(g_mlp, 0)

            dve.wait_ge(n_r, 2)
            with dve.Fori(0, ROUNDS) as i:
                for e in range(4):
                    n = N_D + e + 4 * i
                    split_low(n + 1, (N_D + e + 1) % 2)
                    for c, (t0, tw) in enumerate(CHUNKS):
                        if e < 2:
                            buf = utmp[:, (3 * e + c) % 2, 0:tw]
                            chunk_done(n, c)
                            v_.scalar_tensor_tensor(out=buf, in0=bank[c][:, 0:tw], scalar=0.0, in1=r_bc[:, t0:t0 + tw],
                                                    op0=ALU.max, op1=ALU.mult).then_inc(evac, 1)
                            dve.wait_ge(u_high, 6 * i + 3 * e + c + 2)
                            v_.tensor_tensor(u_lo[:, e, t0:t0 + tw], buf, u_hi[:, e, t0:t0 + tw].bitcast(F32),
                                             ALU.subtract).then_inc(u_low, 1)
                            continue
                        for jt in range(4):
                            if jt < 3:
                                dve.wait_ge(w2_done, 18 * i + 9 * (e - 2) + 3 * c + jt + 2)
                            else:
                                chunk_done(n, c)
                            x = xres[:, 4 * (e - 2) + jt, t0:t0 + tw]
                            v_.tensor_tensor(x, bank[3 + jt][:, 0:tw], x, ALU.add).then_inc(w2_read if jt < 3 else evac, 1)

            norm_rows(g_ple, 3 * KT)
            for i in range(KT // 2):
                row = 14 + 2 * (i % 2)
                dve.wait_ge(x1_sq, KT + 2 * i + 3)
                v_.tensor_tensor(work[:, row, :], work[:, row, :], work[:, row + 1, :], ALU.add).then_inc(x1_acc, 1)
            for i in range(5):
                dve.wait_ge(p_high, i + 2)
                v_.tensor_tensor(u_lo[:].rearrange("p a t -> p (a t)")[:, 512 * i:512 * i + 512], bank[6 + i % 2][:],
                                 u_hi[:].rearrange("p a t -> p (a t)")[:, 512 * i:512 * i + 512].bitcast(F32),
                                 ALU.subtract).then_inc(p_low, 1)
            dve.wait_ge(n_r, 3)

            def gate_tile(j, last):
                n = N_E + 2 * j
                split_low(n + 1, (N_E + 1) % 2, 256)
                for c, (t0, tw) in enumerate(CHUNKS):
                    row = work[:, 17, t0:t0 + tw]
                    chunk_done(n, c)
                    if c == 0:
                        dve.wait_ge(yt_done, 3 * j + 1)
                    v_.tensor_tensor(row, bank[c][:, 0:tw], r_bc[:, t0:t0 + tw], ALU.mult).then_inc(evac, 1)
                if not last:
                    split_low(n + 2, N_E % 2)
                for c, (t0, tw) in enumerate(CHUNKS):
                    row = work[:, 17, t0:t0 + tw]
                    chunk_done(n + 1, c)
                    dve.wait_ge(pg_sig, 3 * j + c + 2)
                    v_.tensor_tensor(row, bank[c][:, 0:tw], row, ALU.mult).then_inc(evac, 1)
                    dve.wait_ge(evac, slab_chunks(n + 1) + c + 2)
                    x = xres[:, bass.ds(j, 1), t0:t0 + tw].rearrange("p o t -> p (o t)")
                    v_.tensor_tensor(row, x, row, ALU.add).then_inc(y_ready, 1)

            with dve.Fori(0, KT - 1) as j:
                gate_tile(j, False)
            gate_tile(KT - 1, True)


_INS = ["x_prompt", "x_sample", "p_prompt", "p_sample", "norm_mix_g", "w_in", "gla_wa2_f", "gla_ba_f", "gla_wa2_b",
        "gla_ba_b", "gla_norm_g", "attn_qnorm_g", "attn_knorm_g", "w_branch_a", "w_branch_b", "w_out", "norm_mlp_g",
        "w_mlp1", "w_mlp2", "norm_ple_g", "w_ple_gate", "w_ple_proj"]


def kernel(**inputs):
    import numpy as _np
    import concourse.bacc as _bacc
    from concourse import mybir as _mybir
    from concourse.bass_utils import run_bass_kernel_spmd as _run

    nc = _bacc.Bacc("TRN2", target_bir_lowering=False, num_devices=1)
    arrays, aps = {}, {}
    for name in _INS:
        x = _np.ascontiguousarray(inputs[name])
        arrays[f"in_{name}_dram"] = x
        aps[name] = nc.dram_tensor(f"in_{name}_dram", x.shape, _mybir.dt.from_np(x.dtype), kind="ExternalInput").ap()
    outs = []
    for name in ("x_prompt", "x_sample"):
        outs.append(nc.dram_tensor(f"out_{name}_dram", inputs[name].shape, _mybir.dt.float32, kind="ExternalOutput").ap())
    encoder(nc, aps, *outs)
    r = _run(nc, [arrays], core_ids=[0])
    return r.results[0]["out_x_prompt_dram"], r.results[0]["out_x_sample_dram"]
```

```python
from contextlib import ExitStack

import concourse.bass as bass
from concourse import mybir

ALU = mybir.AluOpType
ACT = mybir.ActivationFunctionType
F32 = mybir.dt.float32
FR = mybir.dt.float32r
U8 = mybir.dt.uint8
I32 = mybir.dt.int32
P = 128

MAP_BYTES = 212736
EPS = 1e-6
MASKED = 1e32


class Chain:

    def __init__(self):
        self.n, self.base = 0, 0

    def value(self):
        self.n += 1
        return self.base + self.n + 1

    def enter(self, i, per):
        self.before, self.per, self.n = self.n, per, 0
        self.base = self.base + self.before + i * per

    def leave(self, times, start):
        assert self.n == self.per, (self.n, self.per)
        self.base, self.n = start + times * self.per, 0


def encoder(nc, a, out_p, out_s):
    D = a["x_sample"].shape[2]
    TS, TP = a["x_sample"].shape[1], a["x_prompt"].shape[1]
    T = TS + TP
    KT = D // P
    NT = T // P
    H = 4
    DK, DV = 128, 256
    RANK = a["gla_wa2_f"].shape[0]
    CHUNKS = [(0, 512), (512, 512), (1024, 256)]
    FF = a["w_mlp1"].shape[1]
    PLE = a["p_sample"].shape[3]
    BLK = NT
    C_GQ = 0
    C_GK = C_GQ + H * DK
    C_GV = C_GK + H * DK
    C_GG = C_GV + H * DV
    C_LR = C_GG + H * DV
    C_AQ = C_LR + 2 * RANK
    C_AK = C_AQ + 3 * H * P
    C_AV = C_AK + 3 * H * P
    C_GATE = C_AV + 3 * H * P
    SLOTS = 18
    N_HEAD = 1
    N_REST = N_HEAD + H * SLOTS
    REST = 2 * KT - 3 * H
    N_C1 = N_REST + REST
    N_C2 = N_C1 + 2 * KT
    N_D = N_C2 + KT
    ROUNDS = FF // (2 * P)
    N_E = N_D + 4 * ROUNDS

    def slab_chunks(n):
        return 3 * n

    with ExitStack() as ctx:
        first = {}

        def sem(name, start=1):
            s = ctx.enter_context(nc.semaphore(name))
            first[s] = start
            return s

        base = (nc.sbuf_base + 31) // 32 * 32
        ctx.enter_context(nc.sbuf_tensor("whole_map", [P, MAP_BYTES // 4], F32))
        ROW = T * 4
        O_HLO = KT * ROW
        O_WHI = 2 * KT * ROW
        O_WLO = O_WHI + 8192
        O_RAW = O_WLO + 8192
        O_WORK = O_RAW + 4096
        O_SMALL = O_WORK + 18 * ROW

        def at(name, shape, dt, off):
            return nc.alloc_sbuf_tensor_at(name, shape, dt, offset=base + off)

        act_hi = at("act_hi", [P, KT, T], FR, 0)
        act_lo = at("act_lo", [P, KT, T], FR, O_HLO)
        w_hi = at("w_hi", [P, 2, 1024], FR, O_WHI)
        w_lo = at("w_lo", [P, 2, 1024], FR, O_WLO)
        w_raw = at("w_raw", [P, 1024], F32, O_RAW)
        work = at("work", [P, 18, T], F32, O_WORK)
        z = work[:, 0:6, :]
        ar = work[:, 6:18, :]
        x_in = at("x_in", [P, NT, 1024], F32, O_WORK)
        x_sq = at("x_sq", [P, 1024], F32, O_WORK + 8 * ROW)
        sq_hi = at("sq_hi", [P, 2, T], FR, O_WORK + 6 * ROW)
        sq_lo = at("sq_lo", [P, T], FR, O_WORK + 16 * ROW)
        ob_hi = at("ob_hi", [P, 4, T], FR, O_WORK)
        ob_lo = at("ob_lo", [P, 4, T], FR, O_WORK + 4 * ROW)
        merged = work[:, 8:16, :]
        xres = work[:, 0:8, :]
        u_hi = at("u_hi", [P, 2, T], FR, O_WORK + 8 * ROW)
        u_lo = at("u_lo", [P, 2, T], FR, O_WORK + 10 * ROW)
        pos = [O_SMALL]

        def small(name, shape, dt=F32):
            size = 1
            for s in shape[1:]:
                size *= s
            size *= 1 if dt == U8 else 4
            t = at(name, shape, dt, pos[0])
            pos[0] += (size + 31) // 32 * 32
            return t

        shared = pos[0]
        pr = at("pr", [P, 2, 256], F32, shared)
        prt = at("prt", [P, 2, 256], F32, shared + 2048)
        bias_w = at("bias_w", [P, 256], F32, shared + 4096)
        bias_b = at("bias_b", [P, P], F32, shared + 5120)
        amat = at("amat", [P, 2, P], F32, shared)
        kdn = at("kdn", [P, 2, 2, P], F32, shared + 1024)
        state = at("state", [P, 2, 2, DV], F32, shared + 3072)
        x_next = at("x_next", [P, T], F32, shared)
        utmp = at("utmp", [P, 2, 512], F32, shared)
        pos[0] = shared + 7168
        dist_w = small("dist_w", [P, 256])
        dist_2 = small("dist_2", [P, P])
        dist_8 = small("dist_8", [P, P])
        ident = small("ident", [P, P])
        ones_r = small("ones_r", [P, P], FR)
        ones = ones_r[:].bitcast(F32)
        mask_b = small("mask_b", [P, P], U8)
        r_bc = at("r_bc", [P, T], F32, pos[0])
        lowrank = small("lowrank", [48, T])
        wa2 = small("wa2", [48, DK])
        ba = small("ba", [P, 2])
        st = small("st", [P, 2 * BLK])
        st_t = small("st_t", [2 * BLK, P])
        cst = small("cst", [P, 6, NT])
        cw = small("cw", [P, 4, NT])
        ebl = small("ebl", [P, 2, T // 64])
        ebt = small("ebt", [P, 2, NT])
        slopes = small("slopes", [P, 3 * H])
        slope = small("slope", [P, 3])
        g_mix = small("g_mix", [P, KT])
        g_mlp = small("g_mlp", [P, KT])
        g_ple = small("g_ple", [P, KT])
        g_gla = small("g_gla", [P, 2])
        g_q = small("g_q", [P, 3])
        g_k = small("g_k", [P, 3])
        eps = small("eps", [P, 1])
        half = small("half", [P, 4])
        ssx = small("ssx", [P, NT])
        rx = small("rx", [P, NT])
        assert pos[0] <= MAP_BYTES, pos[0]

        bank = [ctx.enter_context(nc.psum_tensor(f"bank{i}", [P, 512], F32)) for i in range(8)]

        def dram(name, shape):
            return nc.dram_tensor(name, shape, F32, kind="Internal").ap()

        oa_d = dram("oa_scratch", [H * DV, T])
        ob_d = dram("ob_scratch", [H * P, T])
        gate_d = dram("gate_scratch", [2 * D, T])
        stat_d = dram("stat_scratch", [2, 3, T])
        wgt_d = dram("weight_scratch", [3, T])
        unused_d = dram("unused_scratch", [D])

        w_in = a["w_in"].rearrange("(k p) n -> p k n", p=P)
        w_a = a["w_branch_a"].rearrange("(k p) n -> p k n", p=P)
        w_b = a["w_branch_b"].rearrange("(k p) n -> p k n", p=P)
        w_o = a["w_out"].rearrange("(k p) n -> p k n", p=P)
        w_1 = a["w_mlp1"].rearrange("(k p) n -> p k n", p=P)
        w_2 = a["w_mlp2"].rearrange("(f k p) n -> p f k n", p=P, k=2)
        w_pg = a["w_ple_gate"].rearrange("(k p) n -> p k n", p=P)
        w_pp = a["w_ple_proj"].rearrange("(k p) n -> p k n", p=P)
        x_s = a["x_sample"].rearrange("o t d -> (o t) d")
        x_p = a["x_prompt"].rearrange("o t d -> (o t) d")
        p_s = a["p_sample"].rearrange("l o t d -> (l o t) d")
        p_p = a["p_prompt"].rearrange("l o t d -> (l o t) d")
        y_s = out_s.rearrange("o t d -> (o t) d")
        y_p = out_p.rearrange("o t d -> (o t) d")

        primed = sem("primed")
        const_dma = sem("const_dma", 0)
        ident_ready = sem("ident_ready", 0)
        half_ready = sem("half_ready", 0)
        const_pool = sem("const_pool")
        const_dve = sem("const_dve")
        pool_own, dve_own, act_own = sem("pool_own"), sem("dve_own"), sem("act_own")
        sp_passed, pool_passed, act_passed, dve_passed = (
            sem("sp_passed"), sem("pool_passed"), sem("act_passed"), sem("dve_passed"))
        w_zero = sem("w_zero", 0)
        w_loaded = sem("w_loaded", 0)
        w_high = sem("w_high")
        w_split = sem("w_split")
        mm_done = sem("mm_done")
        evac = sem("evac")
        x_loaded = [sem(f"x_loaded{t}", 0) for t in range(NT)]
        x_sumsq, x_r, x_norm, x_tr, x_high, x_low = (
            sem("x_sumsq", 0), sem("x_r", 0), sem("x_norm", 0), sem("x_tr", 0), sem("x_high", 0), sem("x_low", 0))
        sq_low, sq_ready, ss_done, ln_done, r_ready, qk_ready = (
            sem("sq_low"), sem("sq_ready"), sem("ss_done"), sem("ln_done"), sem("r_ready"), sem("qk_ready"))
        vt_done, vn_ready = sem("vt_done"), sem("vn_ready")
        bias_ready = sem("bias_ready")
        scores_done, max_done, exp_done = sem("scores_done"), sem("max_done"), sem("exp_done")
        prt_done, prt_read, pv_done, o_read = sem("prt_done"), sem("prt_read"), sem("pv_done"), sem("o_read")
        stt_done, stt_read, stat_stored = sem("stt_done"), sem("stt_read"), sem("stat_stored", 16)
        cst_loaded, cexp_in, cexp_out, cw_ready = sem("cst_loaded", 0), sem("cexp_in"), sem("cexp_out"), sem("cw_ready")
        cw_stored, wb_loaded, ob_ready, ob_stored = sem("cw_stored", 16), sem("wb_loaded", 0), sem("ob_ready"), sem("ob_stored", 0)
        gate_stored = sem("gate_stored", 16)
        rest_stored = sem("rest_stored", 0)
        carry_ready = sem("carry_ready")
        head_loaded = sem("head_loaded", 0)
        lr_done, y_read, prep_a, prep_d = sem("lr_done"), sem("y_read"), sem("prep_a"), sem("prep_d")
        cross_ready = sem("cross_ready")
        state_zero = sem("state_zero")
        tile_ready = sem("tile_ready")
        gvt_done, gvn_ready = sem("gvt_done"), sem("gvn_ready")
        pre_done, kdn_ready, a_ready = sem("pre_done"), sem("kdn_ready"), sem("a_ready")
        u_done, s_ready, o_done, go_copied, go_added = (
            sem("u_done"), sem("s_ready"), sem("o_done"), sem("go_copied"), sem("go_added"))
        osq_sum, osq_ready, oss_done, gate_ready, head_done, oa_stored = (
            sem("osq_sum"), sem("osq_ready"), sem("oss_done"), sem("gate_ready"), sem("head_done"), sem("oa_stored", 16))
        ob_loaded, oa_loaded = sem("ob_loaded", 0), sem("oa_loaded", 0)
        c_high, c_low = sem("c_high"), sem("c_low")
        g_loaded, g_sig = sem("g_loaded", 0), sem("g_sig")
        yb_done, yb_read, m_done = sem("yb_done"), sem("yb_read"), sem("m_done")
        m_high, m_low = sem("m_high"), sem("m_low")
        xn_loaded = [sem("xn_loaded0", 0), sem("xn_loaded1", 0)]
        x1_sq, x1_acc, x1_ss, n_ln, n_r, n_high, n_low = (
            sem("x1_sq"), sem("x1_acc"), sem("x1_ss"), sem("n_ln"), sem("n_r"), sem("n_high"), sem("n_low"))
        u_act, u_sq, u_high, u_low = sem("u_act"), sem("u_sq"), sem("u_high"), sem("u_low")
        w2_done, w2_read = sem("w2_done"), sem("w2_read")
        p_loaded, p_tr, p_high, p_low = sem("p_loaded", 0), sem("p_tr"), sem("p_high"), sem("p_low")
        pg_r, pg_sig, pp_done, y_ready, yt_done, yt_read, y_stored = (
            sem("pg_r"), sem("pg_sig"), sem("pp_done"), sem("y_ready"), sem("yt_done"), sem("yt_read"), sem("y_stored", 16))

        def seqs(row):
            return row[:, 0:TS], row[:, TS:T]

        def queries(row, g, b):
            s, p = seqs(row)
            if g == 0:
                return s[:, P * b:P * b + P] if b < 8 else p[:, P * (b - 8):P * (b - 7)]
            if g == 1:
                if b < 8:
                    return s.rearrange("p (l r) -> p r l", r=4)[:, b % 4, P * (b // 4):P * (b // 4) + P]
                return p.rearrange("p (l r) -> p r l", r=4)[:, 2 * (b - 8):2 * (b - 7), :]
            if b < 8:
                return s.rearrange("p (l r) -> p r l", r=16)[:, 2 * b:2 * b + 2, :]
            return p.rearrange("p (l r) -> p r l", r=16)[:, 8 * (b - 8):8 * (b - 7), :]

        def window(g, b):
            if g == 0:
                ln, l0 = (TS, P * b) if b < 8 else (TP, P * (b - 8))
            elif g == 1 and b < 8:
                ln, l0 = TS // 4, P * (b // 4)
            else:
                return None
            return l0, max(0, l0 - 64), min(ln, l0 + 192), ln

        def block_at(g, b):
            return TS // 4 * (b % 4) + P * (b // 4) if g == 1 and b < 8 else P * b

        def keys(row, g, b):
            w = window(g, b)
            if w is None:
                return row[:, P * b:P * b + P]
            seq = (0 if b < 8 else TS) if g == 0 else TS // 4 * (b % 4)
            return row[:, seq + w[1]:seq + w[2]]

        def by_residue(row, g, c):
            dil = (1, 4, 16)[g]
            s, p = seqs(row)
            if c == 2:
                return p.rearrange("p (r l) -> p r l", r=dil)
            n = 512 // dil
            return s.rearrange("p (r l) -> p r l", r=dil)[:, :, c * n:c * n + n]

        def value_tile(g, m):
            if g == 0 and m in (0, 8):
                s0, s1 = (0, TS) if m == 0 else (TS, T)
            elif g == 1 and m < 8 and m % 2 == 0:
                s0, s1 = TS // 4 * (m // 2), TS // 4 * (m // 2 + 1)
            elif g == 0:
                return [(P * m - 64, P * m + 64)]
            elif g == 1 and m < 8:
                return [(TS // 4 * (m // 2) + 64, TS // 4 * (m // 2) + 192)]
            else:
                return [(P * m, P * m + P)]
            return [(s1 - P, s1), (s0, s0 + 64)]

        def pieces(g, b):
            w = window(g, b)
            if w is None:
                return [(b, 0, P, 0)]
            l0, lo, hi, ln = w
            if g == 0:
                edge, mid = (0, b) if b < 8 else (8, 9)
                before, behind = (mid, mid + 1) if b < 8 else (9, 9)
            else:
                edge = 2 * (b % 4)
                before = behind = edge + 1
            if l0 == 0:
                return [(edge, 0, 64, 0), (behind, 0, P, 64)]
            if hi == ln:
                return [(before, 0, P, 0), (edge, 64, P, 64)]
            return [(before, 0, P, 0), (behind, 0, P, P)]

        def like(flat, shaped):
            if len(shaped.shape) == 3:
                return flat.rearrange("p (j l) -> p j l", j=shaped.shape[1])
            return flat

        def x_row(e):
            return work[:, 17, :] if e else x_next[:]

        WB = (6, 7, 9)
        carry = ar[:, 8, :].rearrange("p (c l) -> p c l", l=64)
        keyvals = work[:, 12:14, :].rearrange("p a t -> p (a t)").rearrange("p (n v) -> p n v", v=DV)
        k_cross = ar[:, 10, :].rearrange("p (d t l) -> p d t l", d=2, l=64)
        q_second = ar[:, 11, :].rearrange("p (d t l) -> p d t l", d=2, l=64)
        o_gla = ar[:, 8:10, :]
        T_BLOCK, BSTEP = 6, 4
        T_STAT = T_BLOCK + BSTEP * BLK
        T_LR = (268, 287)
        T_DECAY = (277, 316)
        T_QK = (281, 328)
        T_SPAN = 334
        T_CW = 272
        T_COMBINE = 292
        T_VT = (321, 325, 329, 333, 341)
        T_GLA, GSTEP = 348, 6
        T_OUT = T_GLA + GSTEP * NT
        X_TILES = [(t0 // P, (t0 + tw) // P) for t0, tw in CHUNKS]
        REST_ROWS = (16, 17, 0, 1)
        Z_OF = [0, 1, 2, 3, 4, 5, 0, 1, 2, 3, 4, 5, 0, 1, 2, 3, 4, 5]

        ctx.enter_context(nc.allow_non_contiguous_dma(reason="small vectors and softmax statistics"))
        block = ctx.enter_context(nc.Block())

        @block.sync
        def _(sp):
            def load(n, src, width=1024, first=False):
                if not first:
                    sp.wait_ge(w_split, n + 1)
                    sp.sem_inc(sp_passed, 1)
                sp.dma_start(w_raw[:, 0:width].rearrange("p (k n) -> p k n", n=src.shape[2]), src).then_inc(w_loaded, 16)

            for t in range(NT):
                src, row = (x_s, t * P) if t < TS // P else (x_p, t * P - TS)
                sp.dma_start(x_in[:, t, :], src[row:row + P, :]).then_inc(x_loaded[t], 16)
            sp.wait_ge(primed, 1)
            with sp.Fori(0, H) as h:
                n = N_HEAD + h * SLOTS
                cols = []
                for g in range(3):
                    cols += [C_AK + g * H * P + h * P, C_AQ + g * H * P + h * P, C_AV + g * H * P + h * P]
                cols += [C_GK + h * DK, C_GQ + h * DK, C_GV + h * DV, C_GV + P + h * DV, C_GG + h * DV, C_GG + P + h * DV]
                cols += [C_GATE + j * P + h * (3 * P) for j in range(3)]
                for t, c in enumerate(cols):
                    load(n + t, w_in[:, :, bass.ds(c, P)])
            for j in range(REST):
                c = C_GATE + (3 * H + j) * P
                load(N_REST + j, w_in[:, :, c:c + P])
            with sp.Fori(0, KT) as j:
                load(N_C1 + 2 * j, w_a[:, :, bass.ds(j * P, P)])
                load(N_C1 + 1 + 2 * j, w_b[:, :, bass.ds(j * P, P)], 512)
            with sp.Fori(0, KT) as j:
                load(N_C2 + j, w_o[:, :, bass.ds(j * P, P)])
            with sp.Fori(0, ROUNDS) as i:
                for e in range(2):
                    load(N_D + e + 4 * i, w_1[:, :, bass.ds(i * (2 * P) + e * P, P)])
                for e in range(2):
                    load(N_D + 2 + e + 4 * i, w_2[:, i, :, 512 * e:512 * e + 512])
            with sp.Fori(0, KT) as j:
                load(N_E + 2 * j, w_pg[:, :, bass.ds(j * P, P)])
                load(N_E + 1 + 2 * j, w_pp[:, :, bass.ds(j * P, P)], 256)

        @block.gpsimd
        def _(pool):
            own = Chain()
            nc.gpsimd.memset(ident[:], 0.0).then_inc(ident_ready, 1)
            pool.wait_ge(ident_ready, 1)
            nc.gpsimd.affine_select(out=ident[:], in_=ident[:], compare_op=ALU.not_equal, fill=1.0, base=0,
                                    pattern=[[-1, P]], channel_multiplier=1).then_inc(ident_ready, 1)
            nc.gpsimd.memset(eps[:], EPS)
            nc.gpsimd.memset(half[:], -0.5).then_inc(half_ready, 1)
            for i, (s, start) in enumerate(first.items()):
                if start == 1 and s is not primed:
                    pool.sem_inc(s, 1)
                if start == 16:
                    pool.dma_start(unused_d[i:i + 1], a["norm_mix_g"][0:1]).then_inc(s, 16)
            pool.wait_ge(half_ready, 1)
            for t0, t1 in X_TILES:
                pool.wait_ge(x_sumsq, t1)
                nc.gpsimd.tensor_scalar(rx[:, t0:t1], ssx[:, t0:t1], 1.0 / D, EPS, ALU.mult, ALU.add).then_inc(pool_own, 1)
                pool.wait_ge(pool_own, own.value())
                nc.gpsimd.tensor_tensor(rx[:, t0:t1], rx[:, t0:t1], half[:, 0:t1 - t0], ALU.pow).then_inc(x_r, 1)
                if t0 == 0:
                    for s, start in first.items():
                        if start == 16:
                            pool.wait_ge(s, 16)
                    pool.sem_inc(primed, 1)

            for k in range(3 * H):
                nc.gpsimd.memset(slopes[:, k:k + 1], 2.0 ** (-8.0 * (k % 3 * H + k // 3 + 1) / (3 * H)) * (1, 4, 16)[k % 3]).then_inc(pool_own, 1)
                pool.wait_ge(pool_own, own.value())
                pool.sem_inc(pool_passed, 1)
            iot = ar[:, 11, 0:256]
            neg = ar[:, 11, 256:512]

            def distance(first):
                nc.gpsimd.iota(iot, [[1, 256]], base=first, channel_multiplier=-1, allow_small_or_imprecise_dtypes=True).then_inc(pool_own, 1)
                pool.wait_ge(pool_own, own.value())
                pool.sem_inc(pool_passed, 1)
                nc.gpsimd.tensor_scalar(neg, iot, -1.0, None, ALU.mult).then_inc(pool_own, 1)
                pool.wait_ge(pool_own, own.value())
                pool.sem_inc(pool_passed, 1)
                nc.gpsimd.affine_select(out=iot, in_=iot, compare_op=ALU.is_ge, fill=0.0, base=first,
                                        pattern=[[1, 256]], channel_multiplier=-1).then_inc(pool_own, 1)
                pool.wait_ge(pool_own, own.value())
                pool.sem_inc(pool_passed, 1)
                nc.gpsimd.affine_select(out=neg, in_=neg, compare_op=ALU.is_ge, fill=0.0, base=-first,
                                        pattern=[[-1, 256]], channel_multiplier=1).then_inc(pool_own, 1)
                pool.wait_ge(pool_own, own.value())
                pool.sem_inc(pool_passed, 1)

            distance(-64)
            nc.gpsimd.tensor_tensor(dist_w[:], iot, neg, ALU.add).then_inc(pool_own, 1)
            pool.wait_ge(pool_own, own.value())
            pool.sem_inc(pool_passed, 1)
            nc.gpsimd.affine_select(out=dist_w[:], in_=dist_w[:], compare_op=ALU.is_ge, fill=MASKED, base=128,
                                    pattern=[[-1, 256]], channel_multiplier=1).then_inc(pool_own, 1)
            pool.wait_ge(pool_own, own.value())
            pool.sem_inc(pool_passed, 1)
            nc.gpsimd.affine_select(out=dist_w[:], in_=dist_w[:], compare_op=ALU.is_ge, fill=MASKED, base=0,
                                    pattern=[[1, 256]], channel_multiplier=-1).then_inc(pool_own, 1)
            pool.wait_ge(pool_own, own.value())
            pool.sem_inc(pool_passed, 1)
            distance(0)
            for dst, w in ((dist_2, 64), (dist_8, 16)):
                nc.gpsimd.tensor_tensor(dst[:], iot[:, 0:P], neg[:, 0:P], ALU.add).then_inc(pool_own, 1)
                pool.wait_ge(pool_own, own.value())
                pool.sem_inc(pool_passed, 1)
                v = dst[:].rearrange("p (j l) -> p j l", l=w)
                nc.gpsimd.affine_select(out=v, in_=v, compare_op=ALU.is_ge, fill=MASKED, base=0,
                                        pattern=[[-w, P // w], [0, w]], channel_multiplier=1).then_inc(pool_own, 1)
                pool.wait_ge(pool_own, own.value())
                pool.sem_inc(pool_passed, 1)
                nc.gpsimd.affine_select(out=v, in_=v, compare_op=ALU.is_ge, fill=MASKED, base=w - 1,
                                        pattern=[[w, P // w], [0, w]], channel_multiplier=-1).then_inc(pool_own, 1)
                pool.wait_ge(pool_own, own.value())
                pool.sem_inc(pool_passed, 1)
            m = ar[:, 11, 512:640]
            nc.gpsimd.memset(m, 1.0).then_inc(pool_own, 1)
            pool.wait_ge(pool_own, own.value())
            nc.gpsimd.affine_select(out=m, in_=m, compare_op=ALU.is_gt, fill=0.0, base=0,
                                    pattern=[[-1, P]], channel_multiplier=1).then_inc(pool_own, 1)
            pool.wait_ge(pool_own, own.value())
            nc.gpsimd.tensor_copy(mask_b[:], m).then_inc(pool_own, 1)
            pool.wait_ge(pool_own, own.value())
            pool.sem_inc(const_pool, 1)

            def store_gate(n, zrow, rows, stored):
                pool.wait_ge(evac, slab_chunks(n + 1) + 1)
                pool.sem_inc(pool_passed, 1)
                pool.dma_start(gate_d[rows, :], work[:, zrow, :]).then_inc(stored, 16)

            def store_stats(h, g):
                pool.wait_ge(stt_read, 3 * h + g + 2)
                pool.sem_inc(pool_passed, 1)
                for mz in range(2):
                    r0 = mz * BLK
                    s = stat_d[mz, g, 0:TS]
                    p = stat_d[mz, g, TS:T]
                    if g == 0:
                        todo = [(st_t[r0:r0 + 10, :], stat_d[mz, g, :].rearrange("(b q) -> b q", q=P))]
                    elif g == 1:
                        sv = s.rearrange("(f l r) -> f r l", r=4, l=P)
                        todo = [(st_t[r0 + 4 * f:r0 + 4 * f + 4, :], sv[f]) for f in range(2)]
                        todo.append((st_t[r0 + 8:r0 + 10, :].rearrange("b (j l) -> b j l", j=2),
                                     p.rearrange("(l b j) -> b j l", b=2, j=2)))
                    else:
                        todo = [(st_t[r0:r0 + 8, :].rearrange("b (j l) -> b j l", j=2),
                                 s.rearrange("(l b j) -> b j l", b=8, j=2)),
                                (st_t[r0 + 8:r0 + 10, :].rearrange("b (j l) -> b j l", j=8),
                                 p.rearrange("(l b j) -> b j l", b=2, j=8))]
                    for src, dst in todo:
                        pool.dma_start(dst, src).then_inc(stat_stored, 16)

            start = own.base + own.n
            with pool.Fori(0, H) as h:
                own.enter(h, 2)
                pool.wait_ge(head_done, h + 1)
                pool.sem_inc(pool_passed, 1)
                for d, (w2, b2) in enumerate((("gla_wa2_f", "gla_ba_f"), ("gla_wa2_b", "gla_ba_b"))):
                    pool.dma_start(wa2[32 * d:32 * d + RANK, :], a[w2][:, bass.ds(h * DK, DK)]).then_inc(head_loaded, 16)
                    pool.dma_start(ba[:, d:d + 1], a[b2].rearrange("(n o) -> n o", o=1)[bass.ds(h * DK, DK), :]
                                   ).then_inc(head_loaded, 16)
                pool.wait_ge(oa_stored, 32 * h + 16)
                pool.sem_inc(pool_passed, 1)
                nc.gpsimd.memset(ar[:, 8, :], 1.0).then_inc(pool_own, 1)
                pool.wait_ge(pool_own, own.value())
                pool.sem_inc(pool_passed, 1)
                nc.gpsimd.memset(carry[:, :, 0:1], 0.0).then_inc(carry_ready, 1)
                for g in range(3):
                    store_stats(h, g)
                pool.wait_ge(stat_stored, 16 * 12 * (h + 1) + 16)
                pool.sem_inc(pool_passed, 1)
                pool.dma_start(cst[:], stat_d.rearrange("m g (p j) -> p (m g) j", j=NT)).then_inc(cst_loaded, 16)
                pool.wait_ge(prep_d, 8 * h + 3)
                pool.sem_inc(pool_passed, 1)
                nc.gpsimd.memset(carry[:, :, 0:1], 1.0).then_inc(pool_own, 1)
                pool.wait_ge(pool_own, own.value())
                pool.sem_inc(pool_passed, 1)
                nc.gpsimd.memset(carry[:, :, 63:64], 0.0).then_inc(carry_ready, 1)
                pool.wait_ge(cw_ready, h + 2)
                pool.sem_inc(pool_passed, 1)
                pool.dma_start(wgt_d.rearrange("g (p j) -> p g j", j=NT), cw[:, 0:3, :]).then_inc(cw_stored, 16)
                pool.wait_ge(cw_stored, 16 * (h + 1) + 16)
                pool.sem_inc(pool_passed, 1)
                for g in range(3):
                    pool.dma_start(ar[:, WB[g], :], wgt_d[g, :].partition_broadcast(P)).then_inc(wb_loaded, 16)
                pool.wait_ge(prt_read, 30 * h + 31)
                pool.wait_ge(pv_done, 30 * h + 31)
                pool.wait_ge(exp_done, 30 * h + 31)
                pool.wait_ge(prt_done, 30 * h + 31)
                pool.wait_ge(max_done, 30 * h + 31)
                pool.sem_inc(pool_passed, 1)
                nc.gpsimd.memset(state[:], 0.0).then_inc(state_zero, 1)
                pool.wait_ge(ob_ready, h + 2)
                pool.sem_inc(pool_passed, 1)
                pool.dma_start(ob_d[bass.ds(h * P, P), :], ar[:, 3, :]).then_inc(ob_stored, 16)
                for j in range(3):
                    store_gate(N_HEAD + h * SLOTS + 15 + j, Z_OF[15 + j], bass.ds(h * (3 * P) + j * P, P), gate_stored)
                pool.wait_ge(head_done, h + 2)
                pool.sem_inc(pool_passed, 1)
                for v in range(2):
                    pool.dma_start(oa_d[bass.ds(h * DV + v * P, P), :], ar[:, 8 + v, :]).then_inc(oa_stored, 16)
            own.leave(H, start)

            pool.wait_ge(oa_stored, 32 * H + 16)
            pool.sem_inc(pool_passed, 1)
            pool.wait_ge(ob_stored, 16 * H)
            pool.sem_inc(pool_passed, 1)
            for k in range(KT):
                pool.dma_start(merged[:, k, :], oa_d[P * k:P * k + P, :]).then_inc(oa_loaded, 16)
            pool.wait_ge(gate_stored, 16 * 3 * H + 16)
            pool.sem_inc(pool_passed, 1)
            for k in range(4):
                pool.dma_start(work[:, 4 + k, :], ob_d[P * k:P * k + P, :]).then_inc(ob_loaded, 16)
            for j in range(REST):
                rows = slice((3 * H + j) * P, (3 * H + j + 1) * P)
                store_gate(N_REST + j, REST_ROWS[j], rows, rest_stored)
            pool.wait_ge(rest_stored, 16 * REST)
            pool.sem_inc(pool_passed, 1)
            def load_x(j, e):
                if isinstance(j, int):
                    if e:
                        pool.wait_ge(m_done, 3 * KT + 1)
                        pool.sem_inc(pool_passed, 1)
                else:
                    pool.wait_ge(mm_done, slab_chunks(N_C2 - 1 + e) + 6 * j + 1)
                    pool.sem_inc(pool_passed, 1)
                dst = x_row(e).rearrange("p (n d) -> p n d", d=P)
                cols = bass.ds(j * (2 * P) + e * P, P)
                pool.dma_start(dst[:, 0:TS // P, :], x_s.rearrange("(n p) d -> p n d", p=P)[:, :, cols]).then_inc(xn_loaded[e], 16)
                pool.dma_start(dst[:, TS // P:NT, :], x_p.rearrange("(n p) d -> p n d", p=P)[:, :, cols]).then_inc(xn_loaded[e], 16)

            load_x(0, 0)
            with pool.Fori(0, KT) as j:
                pool.wait_ge(m_done, 3 * j + 1)
                pool.sem_inc(pool_passed, 1)
                for e in range(2):
                    pool.dma_start(work[:, 16 + e, :], gate_d[bass.ds(j * P + e * D, P), :]).then_inc(g_loaded, 16)

            load_x(0, 1)
            with pool.Fori(1, KT // 2) as j:
                for e in range(2):
                    load_x(j, e)

            pool.wait_ge(x1_ss, 2)
            pool.sem_inc(pool_passed, 1)
            for e in range(2):
                dst = work[:, 12 + e, :].rearrange("p (n d) -> p n d", d=P)
                for src, n0, n1 in ((p_s, 0, TS // P), (p_p, TS // P, NT)):
                    pool.dma_start(dst[:, n0:n1, :], src.rearrange("(n p) d -> p n d", p=P)[:, :, e * P:e * P + P]
                                   ).then_inc(p_loaded, 16)
            with pool.Fori(0, KT) as j:
                pool.wait_ge(yt_read, 3 * j + 4)
                pool.sem_inc(pool_passed, 1)
                src = work[:, 16, :].rearrange("p (n d) -> p n d", d=P)
                cols = bass.ds(j * P, P)
                for dst, n0, n1 in ((y_s, 0, TS // P), (y_p, TS // P, NT)):
                    pool.dma_start(dst.rearrange("(n p) d -> p n d", p=P)[:, :, cols], src[:, n0:n1, :]
                                   ).then_inc(y_stored, 16)
            pool.wait_ge(y_stored, 32 * KT + 16)
            pool.sem_inc(pool_passed, 1)

        @block.tensor
        def _(pe):
            def ready(n, c):
                if c == 0:
                    pe.wait_ge(w_split, n + 2)
                pe.wait_ge(evac, slab_chunks(n - 1) + c + 2)

            def steps(slot, c, k0, k1, kt, hi, lo, out=None, first=True, column=lambda k: k):
                t0, tw = CHUNKS[c]
                out = bank[c][:, 0:tw] if out is None else out
                for k in range(k0, k1):
                    w0 = column(k) * P
                    wh, wl = w_hi[:, slot, w0:w0 + P], w_lo[:, slot, w0:w0 + P]
                    rh, rl = hi[:, k, t0:t0 + tw], lo[:, k, t0:t0 + tw]
                    nc.tensor.matmul(out, wh, rh, start=first and k == 0, stop=False, skip_group_check=True)
                    nc.tensor.matmul(out, wh, rl, start=False, stop=False, skip_group_check=True)
                    mm = nc.tensor.matmul(out, wl, rh, start=False, stop=k == kt - 1, skip_group_check=True)
                return mm

            def whole(n, slot, kt, hi, lo, inputs=None):
                for c in range(3):
                    ready(n, c)
                    if inputs is not None:
                        inputs(c)
                    steps(slot, c, 0, kt, kt, hi, lo).then_inc(mm_done, 1)

            def transposed_x(c):
                for k in range(KT):
                    q = c * KT + k
                    if k == 0:
                        pe.wait_ge(x_norm, X_TILES[c][1])
                    if q >= 5:
                        pe.wait_ge(x_low, q - 4)
                    for i, t in enumerate(range(*X_TILES[c])):
                        mm = nc.tensor.transpose(bank[3 + q % 5][:, i * P:i * P + P], x_in[:, t, k * P:k * P + P],
                                                 ident[:])
                    mm.then_inc(x_tr, 1)

            def low_rank(c):
                pe.wait_ge(x_low, (c + 1) * KT)
                if c == 0:
                    pe.wait_ge(w_split, 2)
                steps(0, c, 0, KT, KT, act_hi, act_lo).then_inc(mm_done, 1)

            pe.wait_ge(ident_ready, 2)
            transposed_x(0)
            pe.wait_ge(primed, 1)
            transposed_x(1)
            low_rank(0)
            transposed_x(2)
            low_rank(1)
            low_rank(2)

            pe.wait_ge(const_dve, 2)

            def unit_steps(h, g, tau):
                u = 3 * h + g
                kz, qz, vz = (z[:, (3 * (g % 2)) + i, :] for i in range(3))
                if tau in (-22, -12):
                    e = int(tau == -12)
                    pe.wait_ge(sq_low, 2 * u + e + 2)
                    if e == 0:
                        if g == 0:
                            pe.wait_ge(head_done, h + 1)
                        pe.wait_ge(stt_read, u + 1)
                        pe.wait_ge(max_done, 10 * u + 1)
                    else:
                        pe.wait_ge(ln_done, 2 * u + 2)
                    for c, (t0, tw) in enumerate(CHUNKS):
                        nc.tensor.matmul(bank[(3, 4, 7)[c]][:, 0:tw], ones_r[:], sq_hi[:, e, t0:t0 + tw],
                                         start=True, stop=False)
                        mm = nc.tensor.matmul(bank[(3, 4, 7)[c]][:, 0:tw], ones_r[:], sq_lo[:, t0:t0 + tw],
                                              start=False, stop=True)
                    mm.then_inc(ss_done, 1)
                if tau in (4, 5, 9):
                    i = (4, 5, 9).index(tau)
                    if i == 0:
                        pe.wait_ge(evac, slab_chunks(N_HEAD + 3 * g + 3) + h * (3 * SLOTS) + 1)
                        pe.wait_ge(prt_read, 10 * u + 1)
                    elif i == 1:
                        pe.wait_ge(o_read, 10 * u + 1)
                    else:
                        pe.wait_ge(vn_ready, 3 * u + 2)
                    for m in range(4 * i, min(4 * i + 4, BLK)):
                        for c0, c1 in value_tile(g, m):
                            mm = nc.tensor.transpose(bank[6 if i == 1 else 5][0:c1 - c0, (m % 4) * P:(m % 4 + 1) * P],
                                                     vz[:, c0:c1], ident[:])
                    mm.then_inc(vt_done, 1)
                b, at_ = divmod(tau - T_BLOCK, BSTEP)
                if at_ == 0 and 0 <= b < BLK:
                    if b == 0:
                        pe.wait_ge(qk_ready, 2 * u + 3)
                    if b >= 2:
                        pe.wait_ge(max_done, 10 * u + b)
                    kk = keys(kz, g, b)
                    w = window(g, b)
                    nk = P if w is None else w[2] - w[1]
                    q0 = block_at(g, b)
                    nc.tensor.matmul(bank[3 + b % 2][:, 0:nk], qz[:, q0:q0 + P], kk,
                                     start=True, stop=True).then_inc(scores_done, 1)
                if at_ == 1 and 1 <= b <= BLK:
                    b -= 1
                    pe.wait_ge(exp_done, 10 * u + b + 2)
                    if b == 0:
                        pe.wait_ge(vn_ready, 3 * u + 4)
                    else:
                        pe.wait_ge(prt_read, 10 * u + b + 1)
                    for i, (m, p0, p1, c0) in enumerate(pieces(g, b)):
                        mm = nc.tensor.transpose(bank[5][:, i * P:i * P + P], pr[:, b % 2, c0:c0 + P], ident[:])
                    mm.then_inc(prt_done, 1)
                b, at_ = divmod(tau - T_BLOCK - 8, BSTEP)
                if at_ == 0 and 0 <= b < BLK:
                    pe.wait_ge(prt_read, 10 * u + b + 2)
                    if b >= 1:
                        pe.wait_ge(o_read, 10 * u + b + 1)
                    pc = pieces(g, b)
                    for i, (m, p0, p1, c0) in enumerate(pc):
                        mm = nc.tensor.matmul(bank[6][:, 0:P], ar[p0:p1, 2, m * P:m * P + P],
                                              prt[p0:p1, b % 2, i * P:i * P + P], start=i == 0, stop=i == len(pc) - 1)
                    mm.then_inc(pv_done, 1)
                if tau == T_STAT:
                    pe.wait_ge(exp_done, 10 * u + 11)
                    nc.tensor.transpose(bank[7][0:2 * BLK, 0:P], st[:, 0:2 * BLK], ident[:]).then_inc(stt_done, 1)

            def gla_steps(h, tick):
                if tick in T_LR:
                    d = T_LR.index(tick)
                    if d == 0:
                        pe.wait_ge(head_loaded, 64 * (h + 1))
                        pe.wait_ge(stt_read, 3 * h + 4)
                        pe.wait_ge(evac, 4)
                    else:
                        pe.wait_ge(y_read, 2 * h + 2)
                    for c, (t0, tw) in enumerate(CHUNKS):
                        mm = nc.tensor.matmul(bank[(3, 4, 7)[c]][:, 0:tw], wa2[32 * d:32 * d + RANK, :],
                                              lowrank[32 * d:32 * d + RANK, t0:t0 + tw], start=True, stop=True)
                    mm.then_inc(lr_done, 1)
                if tick in T_VT:
                    i = T_VT.index(tick)
                    pe.wait_ge(evac, slab_chunks(N_HEAD + 12) + i // 2 + 2 + h * (3 * SLOTS))
                    if i == 0:
                        pe.wait_ge(o_read, 30 * h + 31)
                    if i >= 2:
                        pe.wait_ge(gvn_ready, 5 * h + i)
                    for q in range(4):
                        src = z[:, 0 if q % 2 else 5, :]
                        tile = 2 * i + q // 2
                        mm = nc.tensor.transpose(bank[5 + i % 2][:, q * P:q * P + P], src[:, tile * P:tile * P + P],
                                                 ident[:])
                    mm.then_inc(gvt_done, 1)

                def prelude(j):
                    if j == 0:
                        pe.wait_ge(tile_ready, h + 2)
                    else:
                        pe.wait_ge(a_ready, 10 * h + j + 1)
                        pe.wait_ge(kdn_ready, 10 * h + j + 1)
                    fw, bw = slice(j * P, j * P + P), slice((NT - 1 - j) * P, (NT - j) * P)
                    c0, c1 = slice(j * P, j * P + 64), slice(j * P + 64, j * P + P)
                    cross = ar[:, 10, :]
                    b0 = (NT + j - 1) * 64
                    for out, keys_, queries_ in (
                            (bank[3][:, 0:P], ar[:, 1, fw], ar[:, 0, fw]),
                            (bank[3][0:64, 64:P], cross[:, j * 64:j * 64 + 64], ar[:, 0, c1]),
                            (bank[3][:, P:P + 64], cross[:, b0:b0 + P], ar[:, 3, c0]),
                            (bank[3][0:64, P:P + 64], ar[:, 4, c0], ar[:, 3, c0]),
                            (bank[3][:, P + 64:2 * P], ar[:, 4, fw], ar[:, 3, c1])):
                        nc.tensor.matmul(out, keys_, queries_, start=True, stop=True, skip_group_check=True)
                    nc.tensor.transpose(bank[3][:, 2 * P:3 * P], ar[:, 2, fw], ident[:])
                    nc.tensor.transpose(bank[3][:, 3 * P:4 * P], ar[:, 5, bw], ident[:]).then_inc(pre_done, 1)

                if tick == T_OUT + 9:
                    pe.wait_ge(osq_sum, h + 2)
                    pe.wait_ge(s_ready, 20 * h + 21)
                    for c, (t0, tw) in enumerate(CHUNKS):
                        nc.tensor.matmul(bank[3 + c][:, 0:tw], ones[:], ar[:, 10, t0:t0 + tw],
                                         start=True, stop=True).then_inc(oss_done, 1)
                if tick == T_GLA - 4:
                    prelude(0)
                j, at_ = divmod(tick - T_GLA, GSTEP)
                if not 0 <= j < NT:
                    return
                jb = NT - 1 - j
                if at_ == 0:
                    pe.wait_ge(kdn_ready, 10 * h + j + 2)
                    if j == 0:
                        pe.wait_ge(gvn_ready, 5 * h + 6)
                        pe.wait_ge(y_read, 2 * h + 3)
                        pe.wait_ge(state_zero, h + 2)
                    else:
                        pe.wait_ge(s_ready, 20 * h + 2 * j + 1)
                    for d, tile in ((0, j), (1, jb)):
                        nc.tensor.matmul(bank[4 + d][:, 0:DV], kdn[:, j % 2, d, :], keyvals[:, tile, :],
                                         start=True, stop=True).then_inc(u_done, 1)
                if at_ == 1:
                    pe.wait_ge(a_ready, 10 * h + j + 2)
                    if 1 <= j <= 5:
                        pe.wait_ge(go_copied, 10 * h + 2 * j + 1)
                    elif j > 5:
                        pe.wait_ge(go_added, 10 * h + 2 * (j - 5) + 1)
                    for v in range(2):
                        nc.tensor.matmul(bank[6][:, v * P:v * P + P], keyvals[:, j, v * P:v * P + P],
                                         amat[:, j % 2, :], start=v == 0, stop=False, skip_group_check=True)
                    for d, tile in ((0, j), (1, jb)):
                        c0, c1 = 64 * d, 64 * (1 - d)
                        for v in range(2):
                            s_v = state[:, d, j % 2, v * P:v * P + P]
                            nc.tensor.matmul(bank[6 + d][:, v * P + c0:v * P + c0 + 64], s_v,
                                             ar[:, 3 * d, tile * P + c0:tile * P + c0 + 64],
                                             start=d == 1 and v == 0, stop=False, skip_group_check=True)
                            mm = nc.tensor.matmul(bank[6 + d][:, v * P + c1:v * P + c1 + 64], s_v,
                                                  q_second[:, d, tile, :], start=False, stop=v == 1,
                                                  skip_group_check=True)
                        mm.then_inc(o_done, 1)
                if at_ == 2 and j + 1 < NT:
                    prelude(j + 1)

            with pe.Fori(0, H) as h:
                for tick in range(24 * SLOTS):
                    t, c, k = tick // 24, tick % 24 // 8, tick % 8
                    if k == 0:
                        if c == 0:
                            pe.wait_ge(w_split, N_HEAD + t + 1 + h * SLOTS + 1)
                        pe.wait_ge(evac, slab_chunks(N_HEAD + t - 1) + c + 1 + h * (3 * SLOTS) + 1)
                    mm = steps((N_HEAD + t) % 2, c, k, k + 1, KT, act_hi, act_lo)
                    if k == 7:
                        mm.then_inc(mm_done, 1)
                    for g in range(3):
                        unit_steps(h, g, tick - 24 * (3 + 3 * g))
                    gla_steps(h, tick)
            for j in range(REST):
                whole(N_REST + j, (N_REST + j) % 2, KT, act_hi, act_lo)

            with pe.Fori(0, KT) as j:
                n = N_C1 + 2 * j
                whole(n, N_C1 % 2, KT, act_hi, act_lo, lambda c: pe.wait_ge(c_low, 8 * c + 9))
                whole(n + 1, (N_C1 + 1) % 2, 4, ob_hi, ob_lo, lambda c: pe.wait_ge(c_low, 24 + 5))

            def column_sums(row, first, last):
                for c, (t0, tw) in enumerate(CHUNKS):
                    mm = nc.tensor.matmul(bank[3 + c][:, 0:tw], ones[:], work[:, row, t0:t0 + tw],
                                          start=first, stop=last, skip_group_check=True)
                return mm

            with pe.Fori(0, KT // 2) as i:
                for e in range(2):
                    n = N_C2 + e + 2 * i
                    xt = x_row(e).rearrange("p (n d) -> p n d", d=P)
                    for c, (t0, tw) in enumerate(CHUNKS):
                        ready(n, c)
                        pe.wait_ge(m_low, 8 * c + 9)
                        if c == 0:
                            pe.wait_ge(xn_loaded[e], 32 * i + 32)
                        for q in range(tw // P):
                            nc.tensor.matmul(bank[c][:, q * P:q * P + P], xt[:, t0 // P + q, :], ident[:],
                                             start=q == 0, stop=False, skip_group_check=True)
                        steps((N_C2 + e) % 2, c, 0, KT, KT, act_hi, act_lo, first=False).then_inc(mm_done, 1)
            pe.wait_ge(head_done, H + 1)
            pe.wait_ge(x1_acc, KT + 2)
            column_sums(8, True, True).then_inc(x1_ss, 1)

            with pe.Fori(0, ROUNDS) as i:
                for e in range(2):
                    whole(N_D + e + 4 * i, (N_D + e) % 2, KT, act_hi, act_lo, lambda c: pe.wait_ge(n_low, 8 * c + 9))
                for e in range(2):
                    n = N_D + 2 + e + 4 * i
                    pe.wait_ge(w_split, n + 2)
                    for c, (t0, tw) in enumerate(CHUNKS):
                        pe.wait_ge(u_low, 6 * i + 3 + c + 2)
                        for jt in range(4):
                            if jt < 3:
                                pe.wait_ge(w2_read, 18 * i + 9 * e + 3 * c + jt + 2)
                            else:
                                pe.wait_ge(evac, slab_chunks(n) + c + 1)
                            mm = steps((N_D + e) % 2, c, 0, 2, 2, u_hi, u_lo, out=bank[3 + jt][:, 0:tw],
                                       column=lambda k: 4 * k + jt)
                            mm.then_inc(mm_done if jt == 3 else w2_done, 1)

            def squares_and_p():
                def transposed_p(i0, i1):
                    for i in range(i0, i1):
                        if i >= 2:
                            pe.wait_ge(p_low, i)
                        for q in range(4):
                            e, m = divmod(4 * i + q, NT)
                            mm = nc.tensor.transpose(bank[6 + i % 2][:, q * P:q * P + P],
                                                     work[:, 12 + e, m * P:m * P + P], ident[:])
                        mm.then_inc(p_tr, 1)

                pe.wait_ge(p_loaded, 64)
                pe.wait_ge(evac, slab_chunks(N_E) + 1)
                transposed_p(0, 2)
                pe.wait_ge(w2_read, 18 * ROUNDS + 4)
                for i in range(KT // 2):
                    pe.wait_ge(x1_acc, KT + 3 + i)
                    column_sums(14 + 2 * (i % 2), i == 0, i == KT // 2 - 1).then_inc(x1_ss, 1)
                transposed_p(2, 5)

            def transposed_y(j):
                for c, (t0, tw) in enumerate(CHUNKS):
                    pe.wait_ge(y_ready, 3 * j + c + 2)
                    for q in range(tw // P):
                        mm = nc.tensor.transpose(bank[5 + c][:, q * P:q * P + P],
                                                 work[:, 17, t0 + q * P:t0 + q * P + P], ident[:])
                    mm.then_inc(yt_done, 1)

            def gate_tile(j, first):
                n = N_E + 2 * j
                for c in range(3):
                    ready(n, c)
                    pe.wait_ge(n_low, 24 + 8 * c + 9)
                    steps(N_E % 2, c, 0, KT, KT, act_hi, act_lo).then_inc(mm_done, 1)
                    if c == 0 and not first:
                        pe.wait_ge(yt_read, 3 * j - 2)
                        transposed_y(j - 1)
                if first:
                    squares_and_p()
                whole(n + 1, (N_E + 1) % 2, 2, u_hi, u_lo, lambda c: pe.wait_ge(p_low, 6))

            gate_tile(0, True)
            pe.wait_ge(n_ln, 4)
            with pe.Fori(1, KT) as j:
                gate_tile(j, False)
            pe.wait_ge(yt_read, 3 * KT - 2)
            transposed_y(KT - 1)

        @block.scalar
        def _(act):
            A = nc.scalar.activation
            own = Chain()

            def split_high(n, slot, width=1024):
                act.wait_ge(w_loaded, 16 * n + 32)
                act.wait_ge(mm_done, slab_chunks(n - 1) + 1)
                A(w_hi[:, slot, 0:width], w_raw[:, 0:width], ACT.Copy).then_inc(w_high, 1)

            def chunk_done(n, c):
                act.wait_ge(mm_done, slab_chunks(n) + c + 2)

            def vector(dst, name):
                act.dma_start(dst[:], a[name].rearrange("(k p) -> p k", p=P)).then_inc(const_dma, 16)

            vector(g_mix, "norm_mix_g")
            act.wait_ge(w_zero, 1)
            lr = w_raw[:].rearrange("p (k n) -> p k n", n=P)
            act.dma_start(lr[:, :, 0:RANK], w_in[:, :, C_LR:C_LR + RANK]).then_inc(w_loaded, 16)
            act.dma_start(lr[:, :, 32:32 + RANK], w_in[:, :, C_LR + RANK:C_LR + 2 * RANK]).then_inc(w_loaded, 16)

            def squares(t):
                act.wait_ge(x_loaded[t], 16)
                if t:
                    act.wait_ge(x_sumsq, t)
                A(x_sq[:], x_in[:, t, :], ACT.Square, accum_out=ssx[:, t:t + 1]).then_inc(x_sumsq, 1)

            def x_highs(c):
                t0, tw = CHUNKS[c]
                for k in range(KT):
                    q = c * KT + k
                    act.wait_ge(x_tr, q + 1)
                    A(act_hi[:, k, t0:t0 + tw], bank[3 + q % 5][:, 0:tw], ACT.Copy, scale=g_mix[:, k:k + 1]
                      ).then_inc(x_high, 1)

            for t in range(4):
                squares(t)
            vector(g_mlp, "norm_mlp_g")
            vector(g_ple, "norm_ple_g")
            vector(g_gla, "gla_norm_g")
            act.dma_start(g_q[:], a["attn_qnorm_g"].rearrange("g p -> p g")).then_inc(const_dma, 16)
            act.dma_start(g_k[:], a["attn_knorm_g"].rearrange("g p -> p g")).then_inc(const_dma, 16)
            for t in range(4, 8):
                squares(t)
            act.wait_ge(primed, 1)
            act.wait_ge(w_loaded, 32)
            A(w_hi[:, 0, :], w_raw[:], ACT.Copy).then_inc(w_high, 1)
            act.wait_ge(const_dma, 96)
            x_highs(0)
            for t in range(8, NT):
                squares(t)
            act.wait_ge(w_loaded, 48)
            A(w_hi[:, 1, :], w_raw[:], ACT.Copy).then_inc(w_high, 1)
            x_highs(1)
            x_highs(2)
            for c, (t0, tw) in enumerate(CHUNKS):
                act.wait_ge(mm_done, c + 2)
                A(lowrank[:, t0:t0 + tw], bank[c][0:48, 0:tw], ACT.Copy).then_inc(evac, 1)

            act.wait_ge(const_pool, 2)
            act.wait_ge(const_dve, 2)

            def unit_steps(h, g, tau):
                u = 3 * h + g
                kz, qz = (z[:, 3 * (g % 2) + i, :] for i in range(2))
                if tau in (-40, -23):
                    e = int(tau == -23)
                    act.wait_ge(evac, slab_chunks(N_HEAD + 3 * g + 1 + e) + h * (3 * SLOTS) + 1)
                    if g == 0 and e == 0:
                        act.wait_ge(head_done, h + 1)
                    act.wait_ge(qk_ready, 2 * u + 1)
                    act.wait_ge(sq_low, 2 * u + e + 1)
                    A(ar[:, 11, :], (kz, qz)[e], ACT.Square).then_inc(act_own, 1)
                    act.wait_ge(act_own, own.value())
                    A(sq_hi[:, e, :], ar[:, 11, :], ACT.Copy).then_inc(sq_ready, 1)
                if tau in (-18, -8):
                    e = int(tau == -8)
                    act.wait_ge(ss_done, 2 * u + e + 2)
                    for c, (t0, tw) in enumerate(CHUNKS):
                        ins = A(ar[:, e, t0:t0 + tw], bank[(3, 4, 7)[c]][:, 0:tw], ACT.Ln, bias=eps[:], scale=1.0 / P)
                    ins.then_inc(ln_done, 1)
                if tau == -7:
                    act.wait_ge(ln_done, 2 * u + 3)
                    for e in range(2):
                        A(ar[:, e, :], ar[:, e, :], ACT.Exp, scale=-0.5).then_inc(r_ready, 1)
                b, at_ = divmod(tau - T_BLOCK - 2, BSTEP)
                if at_ == 0 and 0 <= b < BLK:
                    act.wait_ge(max_done, 10 * u + b + 2)
                    w = window(g, b)
                    nk = P if w is None else w[2] - w[1]
                    A(pr[:, b % 2, 0:nk], pr[:, b % 2, 0:nk], ACT.Exp, bias=st[:, b:b + 1], scale=-1.0,
                      accum_out=st[:, BLK + b:BLK + b + 1]).then_inc(exp_done, 1)
                b, at_ = divmod(tau - T_BLOCK - 6, BSTEP)
                if at_ == 0 and 0 <= b < BLK:
                    act.wait_ge(prt_done, 10 * u + b + 2)
                    if b >= 2:
                        act.wait_ge(pv_done, 10 * u + b)
                    w_ = P * len(pieces(g, b))
                    A(prt[:, b % 2, 0:w_], bank[5][:, 0:w_], ACT.Copy).then_inc(prt_read, 1)

            def gla_steps(h, tick):
                if tick == T_CW + 1:
                    act.wait_ge(cexp_in, h + 2)
                    A(cw[:, 0:3, :], cw[:, 0:3, :], ACT.Exp).then_inc(cexp_out, 1)
                if tick - 2 in T_LR:
                    d = T_LR.index(tick - 2)
                    act.wait_ge(lr_done, 2 * h + d + 2)
                    if d == 1:
                        act.wait_ge(prep_a, 6 * h + 4)
                        act.wait_ge(prep_d, 8 * h + 5)
                    for c, (t0, tw) in enumerate(CHUNKS):
                        ins = A(ar[:, 10, t0:t0 + tw], bank[(3, 4, 7)[c]][:, 0:tw], ACT.Identity, bias=ba[:, d:d + 1])
                    ins.then_inc(y_read, 1)
                if tick - 4 in T_LR:
                    d = T_LR.index(tick - 4)
                    act.wait_ge(prep_d, 8 * h + 4 * d + 2)
                    A(ar[:, 11, :], ar[:, 11, :], ACT.Exp).then_inc(act_own, 1)
                    act.wait_ge(act_own, own.value())
                    A(ar[:, 11, :], ar[:, 11, :], ACT.Ln, bias=ones[:, 0:1]).then_inc(prep_a, 1)
                if tick in T_DECAY:
                    d = T_DECAY.index(tick)
                    act.wait_ge(prep_d, 8 * h + 4 * d + 3)
                    if d == 0:
                        act.wait_ge(pv_done, 30 * h + 31)
                        act.wait_ge(qk_ready, 6 * h + 7)
                    else:
                        act.wait_ge(ob_stored, 16 * h + 16)
                        act.wait_ge(ob_ready, h + 2)
                    r = 3 * d
                    A(ar[:, r, :], ar[:, 11, :], ACT.Exp, scale=1.0 / 16).then_inc(act_own, 1)
                    act.wait_ge(act_own, own.value())
                    A(ar[:, r + 1, :], ar[:, 11, :], ACT.Exp, scale=-1.0 / 16).then_inc(prep_a, 1)
                    last = ar[:, 11, :].rearrange("p (c l) -> p c l", l=64)[:, :, 63 * (1 - d)]
                    A(ebl[:, d, :], last, ACT.Exp, scale=1.0 / 16).then_inc(act_own, 1)
                    act.wait_ge(act_own, own.value())
                    act.wait_ge(prep_d, 8 * h + 4 * d + 4)
                    A(ar[:, r + 2, :], ar[:, 10, :], ACT.Exp, scale=1.0 / 16).then_inc(prep_a, 1)

                if tick == T_SPAN:
                    act.wait_ge(prep_d, 8 * h + 9)
                    for e in range(2):
                        kd = ar[:, 3 * e + 2, :].rearrange("p (t c l) -> p t c l", c=2, l=64)
                        A(k_cross[:, e, :, :], kd[:, :, e, :], ACT.Copy).then_inc(cross_ready, 1)

                def decayed(j):
                    act.wait_ge(pre_done, 10 * h + j + 2)
                    if j >= 2:
                        act.wait_ge(u_done, 20 * h + 2 * j - 1)
                    A(kdn[:, j % 2, :, :], bank[3][:, 2 * P:4 * P].rearrange("p (d s) -> p d s", d=2), ACT.Copy
                      ).then_inc(kdn_ready, 1)

                if tick == T_OUT:
                    act.wait_ge(go_added, 10 * h + 11)
                    for v in range(2):
                        A(ar[:, 10 + v, :], o_gla[:, v, :], ACT.Square).then_inc(osq_ready, 1)
                if tick == T_OUT + 2:
                    for v in range(2):
                        A(ar[:, v, :], z[:, 1 + v, :], ACT.Sigmoid).then_inc(gate_ready, 1)
                if tick == T_OUT + 10:
                    act.wait_ge(oss_done, 3 * h + 4)
                    for c, (t0, tw) in enumerate(CHUNKS):
                        A(ar[:, 10, t0:t0 + tw], bank[3 + c][:, 0:tw], ACT.Ln, bias=eps[:], scale=1.0 / DV).then_inc(act_own, 1)
                        act.wait_ge(act_own, own.value())
                    A(ar[:, 10, :], ar[:, 10, :], ACT.Exp, scale=-0.5).then_inc(gate_ready, 1)
                if tick == T_GLA - 3:
                    decayed(0)
                j, at_ = divmod(tick - T_GLA, GSTEP)
                if 0 <= j < NT and at_ == 3 and j + 1 < NT:
                    decayed(j + 1)
                j, at_ = divmod(tick - T_GLA - 3, GSTEP)
                if 0 <= j < 5 and at_ == 0:
                    if j == 0:
                        act.wait_ge(prep_d, 8 * h + 9)
                    for d, tile in ((0, j), (1, NT - 1 - j)):
                        act.wait_ge(o_done, 20 * h + 2 * j + d + 2)
                        A(o_gla[:, :, tile * P:tile * P + P], bank[6 + d][:, 0:DV].rearrange("p (v t) -> p v t", v=2),
                          ACT.Copy).then_inc(go_copied, 1)

            start = own.base + own.n
            with act.Fori(0, H) as h:
                own.enter(h, 15)
                for tick in range(24 * SLOTS + 1):
                    t, r = divmod(tick, 24)
                    if tick % 8 == 0 and tick:
                        tt, c = divmod(tick // 8 - 1, 3)
                        if c == 0:
                            if tt == 0:
                                act.wait_ge(gvt_done, 5 * h + 1)
                            elif tt < 3:
                                act.wait_ge(head_done, h + 1)
                            elif tt < 6:
                                act.wait_ge(gate_stored, 48 * h + 16)
                            elif tt < 15:
                                act.wait_ge(scores_done, 30 * h + 10 * (tt // 3 - 1) + 1)
                            elif tt == 15:
                                act.wait_ge(prep_d, 8 * h + 9)
                            elif tt == 17:
                                act.wait_ge(gvt_done, 5 * h + 6)
                        n = N_HEAD + tt + h * SLOTS
                        t0, tw = CHUNKS[c]
                        chunk_done(n, c)
                        dst, src = work[:, Z_OF[tt], t0:t0 + tw], bank[c][:, 0:tw]
                        if 3 <= tt < 9:
                            dst = by_residue(work[:, Z_OF[tt], :], tt // 3, c)
                            src = src.rearrange("p (l r) -> p r l", r=dst.shape[1])
                        A(dst, src, ACT.Copy, scale=DK ** -0.5 if tt == 9 else 1.0).then_inc(evac, 1)
                    if tick == 24 * SLOTS:
                        break
                    if r == 1:
                        split_high(N_HEAD + t + 1 + h * SLOTS, (N_HEAD + t + 1) % 2)
                    for g in range(3):
                        unit_steps(h, g, tick - 24 * (3 + 3 * g))
                    gla_steps(h, tick)
            own.leave(H, start)

            for j in range(REST):
                split_high(N_REST + j + 1, (N_REST + j + 1) % 2)
                if j == 0:
                    act.wait_ge(head_done, H + 1)
                for c, (t0, tw) in enumerate(CHUNKS):
                    chunk_done(N_REST + j, c)
                    A(work[:, REST_ROWS[j], t0:t0 + tw], bank[c][:, 0:tw], ACT.Copy).then_inc(evac, 1)
                    if j == REST - 1:
                        if c == 0:
                            act.wait_ge(oa_loaded, 16 * KT)
                        for k in range(KT):
                            A(act_hi[:, k, t0:t0 + tw], merged[:, k, t0:t0 + tw], ACT.Copy).then_inc(c_high, 1)
            act.wait_ge(ob_loaded, 64)
            act.wait_ge(rest_stored, 16 * REST)
            for k in range(4):
                A(ob_hi[:, k, :], work[:, 4 + k, :], ACT.Copy).then_inc(c_high, 1)

            with act.Fori(0, KT) as j:
                n = N_C1 + 2 * j
                split_high(n + 1, (N_C1 + 1) % 2, 512)
                for e in range(2):
                    act.wait_ge(g_loaded, 32 * j + 32)
                    A(work[:, 16 + e, :], work[:, 16 + e, :], ACT.Sigmoid).then_inc(g_sig, 1)
                split_high(n + 2, N_C1 % 2)
            for c, (t0, tw) in enumerate(CHUNKS):
                chunk_done(N_C2 - 2, c)
                for k in range(KT):
                    act.wait_ge(m_done, 3 * k + c + 2)
                    A(act_hi[:, k, t0:t0 + tw], merged[:, k, t0:t0 + tw], ACT.Copy).then_inc(m_high, 1)

            act.wait_ge(m_low, 3 * KT + 1)
            with act.Fori(0, KT // 2) as i:
                for e in range(2):
                    n = N_C2 + e + 2 * i
                    split_high(n + 1, (N_C2 + e + 1) % 2)
                    row = work[:, bass.ds(2 * i + e, 1), :].rearrange("p o t -> p (o t)")
                    for c, (t0, tw) in enumerate(CHUNKS):
                        act.wait_ge(mm_done, slab_chunks(n) + c + 2)
                        act.sem_inc(act_passed, 1)
                        A(row[:, t0:t0 + tw], bank[c][:, 0:tw], ACT.Copy).then_inc(evac, 1)
                    act.wait_ge(evac, slab_chunks(n + 1) + 1)
                    act.wait_ge(x1_acc, 2 * i + e + 1)
                    act.sem_inc(act_passed, 1)
                    A(work[:, 12 + e, :], row, ACT.Square).then_inc(x1_sq, 1)

            def norm_rows(gain):
                for c, (t0, tw) in enumerate(CHUNKS):
                    for k in range(KT):
                        A(act_hi[:, k, t0:t0 + tw], xres[:, k, t0:t0 + tw], ACT.Copy, scale=gain[:, k:k + 1]
                          ).then_inc(n_high, 1)

            norm_rows(g_mlp)
            act.wait_ge(x1_ss, 2)
            for c, (t0, tw) in enumerate(CHUNKS):
                A(r_bc[:, t0:t0 + tw], bank[3 + c][:, 0:tw], ACT.Ln, bias=eps[:], scale=1.0 / D).then_inc(w2_read, 1)
            act.wait_ge(w2_read, 4)
            A(r_bc[:], r_bc[:], ACT.Exp, scale=-0.5).then_inc(n_r, 1)

            with act.Fori(0, ROUNDS) as i:
                for e in range(4):
                    n = N_D + e + 4 * i
                    split_high(n + 1, (N_D + e + 1) % 2)
                    if e >= 2:
                        continue
                    for c, (t0, tw) in enumerate(CHUNKS):
                        q = 6 * i + 3 * e + c
                        buf = utmp[:, (3 * e + c) % 2, 0:tw]
                        act.wait_ge(evac, slab_chunks(n) + c + 2)
                        A(buf, buf, ACT.Square).then_inc(u_sq, 1)
                        act.wait_ge(u_sq, q + 2)
                        A(u_hi[:, e, t0:t0 + tw], buf, ACT.Copy).then_inc(u_high, 1)

            chunk_done(N_E - 1, 2)
            act.wait_ge(evac, slab_chunks(N_E) + 1)
            act.wait_ge(w2_read, 18 * ROUNDS + 4)
            norm_rows(g_ple)
            for k in range(KT):
                if k >= 4:
                    act.wait_ge(x1_ss, k // 2 + 1)
                A(work[:, 14 + k % 4, :], xres[:, k, :], ACT.Square).then_inc(x1_sq, 1)
            def p_high_part(i0, i1):
                for i in range(i0, i1):
                    act.wait_ge(p_tr, i + 2)
                    A(u_hi[:].rearrange("p a t -> p (a t)")[:, 512 * i:512 * i + 512], bank[6 + i % 2][:], ACT.Copy
                      ).then_inc(p_high, 1)

            p_high_part(0, 2)
            act.wait_ge(x1_ss, KT // 2 + 2)
            act.wait_ge(n_r, 2)
            for c, (t0, tw) in enumerate(CHUNKS):
                A(r_bc[:, t0:t0 + tw], bank[3 + c][:, 0:tw], ACT.Ln, bias=eps[:], scale=1.0 / D).then_inc(n_ln, 1)
            act.wait_ge(n_ln, 4)
            A(r_bc[:], r_bc[:], ACT.Exp, scale=-0.5).then_inc(n_r, 1)
            p_high_part(2, 5)

            def y_out(j):
                act.wait_ge(y_stored, 32 * j + 16)
                for c, (t0, tw) in enumerate(CHUNKS):
                    act.wait_ge(yt_done, 3 * j + c + 2)
                    A(work[:, 16, t0:t0 + tw], bank[5 + c][:, 0:tw], ACT.Copy).then_inc(yt_read, 1)

            def gate_tile(j, first, last):
                n = N_E + 2 * j
                split_high(n + 1, (N_E + 1) % 2, 256)
                if not first:
                    y_out(j - 1)
                for c, (t0, tw) in enumerate(CHUNKS):
                    act.wait_ge(evac, slab_chunks(n) + c + 2)
                    A(work[:, 17, t0:t0 + tw], work[:, 17, t0:t0 + tw], ACT.Sigmoid).then_inc(pg_sig, 1)
                if not last:
                    split_high(n + 2, N_E % 2)

            gate_tile(0, True, False)
            with act.Fori(1, KT - 1) as j:
                gate_tile(j, False, False)
            gate_tile(KT - 1, False, True)
            y_out(KT - 1)

        @block.vector
        def _(dve):
            v_ = nc.vector
            own = Chain()

            def split_low(n, slot, width=1024):
                dve.wait_ge(w_high, n + 2)
                v_.tensor_tensor(w_lo[:, slot, 0:width], w_raw[:, 0:width], w_hi[:, slot, 0:width].bitcast(F32),
                                 ALU.subtract).then_inc(w_split, 1)

            def chunk_done(n, c):
                dve.wait_ge(mm_done, slab_chunks(n) + c + 2)

            v_.memset(w_raw[:], 0.0).then_inc(w_zero, 1)
            def normed_x(c):
                dve.wait_ge(x_r, c + 1)
                for t in range(*X_TILES[c]):
                    v_.tensor_scalar(x_in[:, t, :], x_in[:, t, :], rx[:, t:t + 1], None, ALU.mult).then_inc(x_norm, 1)

            def x_lows(c):
                t0, tw = CHUNKS[c]
                for k in range(KT):
                    q = c * KT + k
                    dve.wait_ge(x_high, q + 1)
                    v_.scalar_tensor_tensor(out=act_lo[:, k, t0:t0 + tw], in0=bank[3 + q % 5][:, 0:tw],
                                            scalar=g_mix[:, k:k + 1], in1=act_hi[:, k, t0:t0 + tw].bitcast(F32),
                                            op0=ALU.mult, op1=ALU.subtract).then_inc(x_low, 1)

            normed_x(0)
            dve.wait_ge(primed, 1)
            v_.memset(ar[:, 10, 0:P], 1.0).then_inc(dve_own, 1)
            dve.wait_ge(dve_own, own.value())
            v_.tensor_copy(ones_r[:], ar[:, 10, 0:P]).then_inc(dve_own, 1)
            dve.wait_ge(dve_own, own.value())
            dve.wait_ge(const_dma, 96)
            v_.tensor_scalar(g_k[:], g_k[:], -(P ** -0.5), None, ALU.mult).then_inc(const_dve, 1)
            split_low(0, 0)
            normed_x(1)
            x_lows(0)
            normed_x(2)
            split_low(1, 1)
            x_lows(1)
            x_lows(2)

            dve.wait_ge(const_pool, 2)

            def unit_steps(h, g, tau):
                u = 3 * h + g
                kz, qz = (z[:, 3 * (g % 2) + i, :] for i in range(2))
                if tau in (-35, -19):
                    e = int(tau == -19)
                    dve.wait_ge(sq_ready, 2 * u + e + 2)
                    dve.wait_ge(ss_done, 2 * u + e + 1)
                    v_.tensor_tensor(sq_lo[:], ar[:, 11, :], sq_hi[:, e, :].bitcast(F32), ALU.subtract).then_inc(sq_low, 1)
                if tau == -6:
                    dve.wait_ge(max_done, 10 * u + 1)
                    v_.tensor_scalar(bias_w[:], dist_w[:], slope[:, g:g + 1], None, ALU.mult).then_inc(dve_own, 1)
                    dve.wait_ge(dve_own, own.value())
                    if g:
                        v_.tensor_scalar(bias_b[:], dist_2[:], slope[:, g:g + 1], None, ALU.mult).then_inc(dve_own, 1)
                        dve.wait_ge(dve_own, own.value())
                if tau in (6, 7, 10):
                    i = (6, 7, 10).index(tau)
                    m0, m1 = 4 * i, min(4 * i + 4, BLK)
                    dve.wait_ge(vt_done, 3 * u + i + 2)
                    if i == 0 and g:
                        dve.wait_ge(pv_done, 10 * u + 1)
                    v_.tensor_copy(ar[:, 2, m0 * P:m1 * P], bank[6 if i == 1 else 5][:, 0:(m1 - m0) * P]
                                   ).then_inc(vn_ready, 1)
                if tau == -3:
                    for e, (zz, gain) in enumerate(((kz, g_k), (qz, g_q))):
                        dve.wait_ge(r_ready, 2 * u + e + 2)
                        v_.scalar_tensor_tensor(out=zz, in0=zz, scalar=gain[:, g:g + 1], in1=ar[:, e, :],
                                                op0=ALU.mult, op1=ALU.mult).then_inc(qk_ready, 1)
                b, at_ = divmod(tau - T_BLOCK - 1, BSTEP)
                if at_ == 0 and 0 <= b < BLK:
                    if g == 2 and b == 8:
                        dve.wait_ge(max_done, 10 * u + b + 1)
                        v_.tensor_scalar(bias_b[:], dist_8[:], slope[:, g:g + 1], None, ALU.mult).then_inc(dve_own, 1)
                        dve.wait_ge(dve_own, own.value())
                    dve.wait_ge(scores_done, 10 * u + b + 2)
                    if b == 0:
                        dve.wait_ge(stt_done, u + 1)
                        dve.wait_ge(prt_done, 10 * u + 1)
                    if b >= 2:
                        dve.wait_ge(prt_done, 10 * u + b)
                    w = window(g, b)
                    if w is None:
                        nk, bias = P, bias_b[:]
                    else:
                        nk = w[2] - w[1]
                        b0 = w[1] - (w[0] - 64)
                        bias = bias_w[:, b0:b0 + nk]
                    dve.sem_inc(dve_passed, 1)
                    v_.tensor_tensor_reduce(out=pr[:, b % 2, 0:nk], in0=bank[3 + b % 2][:, 0:nk], in1=bias, scale=1.0,
                                            scalar=3e38, op0=ALU.add, op1=ALU.min, accum_out=st[:, b:b + 1]
                                            ).then_inc(max_done, 1)
                b, at_ = divmod(tau - T_BLOCK - 10, BSTEP)
                if at_ == 0 and 0 <= b < BLK:
                    dve.wait_ge(pv_done, 10 * u + b + 2)
                    q = queries(ar[:, 3 + g, :], g, b)
                    v_.tensor_copy(q, like(bank[6][:, 0:P], q)).then_inc(o_read, 1)
                if tau == T_STAT + 2:
                    dve.wait_ge(stt_done, u + 2)
                    dve.wait_ge(stat_stored, 192 * h + 16 * (0, 2, 8)[g] + 16)
                    v_.tensor_copy(st_t[:], bank[7][0:2 * BLK, 0:P]).then_inc(stt_read, 1)

            def gla_steps(h, tick):
                if tick == T_CW:
                    dve.wait_ge(cst_loaded, 16 * h + 16)
                    dve.wait_ge(cw_stored, 16 * h + 16)
                    m = cw[:, 3, :]
                    v_.tensor_tensor(m, cst[:, 0, :], cst[:, 1, :], ALU.min).then_inc(dve_own, 1)
                    dve.wait_ge(dve_own, own.value())
                    v_.tensor_tensor(m, m, cst[:, 2, :], ALU.min).then_inc(dve_own, 1)
                    dve.wait_ge(dve_own, own.value())
                    v_.tensor_tensor(cw[:, 0:3, :], m.unsqueeze(1).broadcast_to([P, 3, NT]), cst[:, 0:3, :],
                                     ALU.subtract).then_inc(cexp_in, 1)
                if tick == T_CW + 3:
                    dve.wait_ge(cexp_out, h + 2)
                    m = cw[:, 3, :]
                    v_.tensor_tensor(cst[:, 3:6, :], cst[:, 3:6, :], cw[:, 0:3, :], ALU.mult).then_inc(dve_own, 1)
                    dve.wait_ge(dve_own, own.value())
                    v_.tensor_tensor(m, cst[:, 3, :], cst[:, 4, :], ALU.add).then_inc(dve_own, 1)
                    dve.wait_ge(dve_own, own.value())
                    v_.tensor_tensor(m, m, cst[:, 5, :], ALU.add).then_inc(dve_own, 1)
                    dve.wait_ge(dve_own, own.value())
                    v_.reciprocal(m, m).then_inc(dve_own, 1)
                    dve.wait_ge(dve_own, own.value())
                    v_.tensor_tensor(cw[:, 0:3, :], cw[:, 0:3, :], m.unsqueeze(1).broadcast_to([P, 3, NT]),
                                     ALU.mult).then_inc(cw_ready, 1)
                if tick == T_COMBINE:
                    dve.wait_ge(wb_loaded, 48 * h + 48)
                    for g in range(3):
                        v_.tensor_tensor(ar[:, 3 + g, :], ar[:, 3 + g, :], ar[:, WB[g], :], ALU.mult).then_inc(dve_own, 1)
                        dve.wait_ge(dve_own, own.value())
                    v_.tensor_tensor(ar[:, 3, :], ar[:, 3, :], ar[:, 4, :], ALU.add).then_inc(dve_own, 1)
                    dve.wait_ge(dve_own, own.value())
                    v_.tensor_tensor(ar[:, 3, :], ar[:, 3, :], ar[:, 5, :], ALU.add).then_inc(ob_ready, 1)
                if tick - 3 in T_LR:
                    d = T_LR.index(tick - 3)
                    dve.wait_ge(y_read, 2 * h + d + 2)
                    if d == 1:
                        dve.wait_ge(prep_a, 6 * h + 4)
                    v_.scalar_tensor_tensor(out=ar[:, 11, :], in0=ar[:, 10, :], scalar=-1.0, in1=ar[:, 10, :],
                                            op0=ALU.mult, op1=ALU.min).then_inc(prep_d, 1)
                if tick - 6 in T_LR:
                    d = T_LR.index(tick - 6)
                    way = slice(None, None, -1) if d else slice(None)
                    dve.wait_ge(prep_a, 6 * h + 3 * d + 2)
                    v_.scalar_tensor_tensor(out=ar[:, 10, :], in0=ar[:, 10, :], scalar=0.0, in1=ar[:, 11, :],
                                            op0=ALU.min, op1=ALU.subtract).then_inc(dve_own, 1)
                    dve.wait_ge(dve_own, own.value())
                    dve.wait_ge(carry_ready, 2 * h + d + 2)
                    v_.tensor_tensor_scan(ar[:, 11, way], ar[:, 8, way], ar[:, 10, way], 0.0, ALU.mult, ALU.add
                                          ).then_inc(prep_d, 1)
                    dve.wait_ge(prep_d, 8 * h + 4 * d + 3)
                    b = ar[:, 11, :].rearrange("p (c l) -> p c l", l=64)
                    e = 63 * (1 - d)
                    v_.tensor_tensor(ar[:, 10, :].rearrange("p (c l) -> p c l", l=64),
                                     b[:, :, e:e + 1].broadcast_to([P, T // 64, 64]), b, ALU.subtract).then_inc(prep_d, 1)
                if tick - 3 in T_VT:
                    i = T_VT.index(tick - 3)
                    dve.wait_ge(gvt_done, 5 * h + i + 2)
                    v_.tensor_copy(keyvals[:, 2 * i:2 * i + 2, :], bank[5 + i % 2][:].rearrange("p (n v) -> p n v", v=DV)
                                   ).then_inc(gvn_ready, 1)
                if tick in T_QK:
                    d = T_QK.index(tick)
                    dve.wait_ge(prep_a, 6 * h + 3 * d + 3)
                    v_.tensor_tensor(ar[:, 3 * d, :], ar[:, 3 * d, :], z[:, 4, :], ALU.mult).then_inc(dve_own, 1)
                    dve.wait_ge(dve_own, own.value())
                    v_.tensor_tensor(ar[:, 3 * d + 1, :], ar[:, 3 * d + 1, :], z[:, 3, :], ALU.mult).then_inc(dve_own, 1)
                    dve.wait_ge(dve_own, own.value())
                    dve.wait_ge(prep_a, 6 * h + 3 * d + 4)
                    last = v_.tensor_tensor(ar[:, 3 * d + 2, :], ar[:, 3 * d + 2, :], z[:, 3, :], ALU.mult)
                    last.then_inc(prep_d, 1)
                if tick == T_SPAN:
                    dve.wait_ge(prep_d, 8 * h + 9)
                    for e in range(2):
                        qe = ar[:, 3 * e, :].rearrange("p (t c l) -> p t c l", c=2, l=64)
                        decay = ebl[:, e, :].rearrange("p (t c) -> p t c", c=2)
                        v_.tensor_tensor(q_second[:, e, :, :], qe[:, :, 1 - e, :],
                                         decay[:, :, e:e + 1].broadcast_to([P, NT, 64]), ALU.mult).then_inc(dve_own, 1)
                        dve.wait_ge(dve_own, own.value())
                    for e in range(2):
                        kd = ar[:, 3 * e + 2, :].rearrange("p (t c l) -> p t c l", c=2, l=64)
                        decay = ebl[:, e, :].rearrange("p (t c) -> p t c", c=2)
                        dve.wait_ge(cross_ready, 2 * h + e + 2)
                        v_.tensor_tensor(kd[:, :, e, :], kd[:, :, e, :],
                                         decay[:, :, 1 - e:2 - e].broadcast_to([P, NT, 64]), ALU.mult).then_inc(dve_own, 1)
                        dve.wait_ge(dve_own, own.value())
                    both = ebl[:].rearrange("p d (t c) -> p d t c", c=2)
                    v_.tensor_tensor(ebt[:], both[:, :, :, 0], both[:, :, :, 1], ALU.mult).then_inc(tile_ready, 1)

                def masked(j):
                    dve.wait_ge(kdn_ready, 10 * h + j + 2)
                    v_.tensor_copy(amat[:, j % 2, :], bank[3][:, 0:P]).then_inc(dve_own, 1)
                    dve.wait_ge(dve_own, own.value())
                    dve.sem_inc(dve_passed, 1)
                    v_.copy_predicated(amat[:, j % 2, :], mask_b[:], bank[3][:, P:2 * P]).then_inc(a_ready, 1)

                if tick == T_OUT + 3:
                    dve.wait_ge(osq_ready, 2 * h + 3)
                    v_.tensor_tensor(ar[:, 10, :], ar[:, 10, :], ar[:, 11, :], ALU.add).then_inc(osq_sum, 1)
                if tick == T_OUT + 6:
                    for v in range(2):
                        dve.wait_ge(gate_ready, 3 * h + v + 2)
                        v_.tensor_tensor(ar[:, v, :], ar[:, v, :], z[:, 1 + v, :], ALU.mult).then_inc(dve_own, 1)
                        dve.wait_ge(dve_own, own.value())
                        v_.scalar_tensor_tensor(out=ar[:, v, :], in0=o_gla[:, v, :], scalar=g_gla[:, v:v + 1],
                                                in1=ar[:, v, :], op0=ALU.mult, op1=ALU.mult).then_inc(dve_own, 1)
                        dve.wait_ge(dve_own, own.value())
                if tick == T_OUT + 13:
                    dve.wait_ge(gate_ready, 3 * h + 4)
                    v_.tensor_tensor(o_gla[:, 0, :], ar[:, 0, :], ar[:, 10, :], ALU.mult).then_inc(dve_own, 1)
                    dve.wait_ge(dve_own, own.value())
                    v_.tensor_tensor(o_gla[:, 1, :], ar[:, 1, :], ar[:, 10, :], ALU.mult).then_inc(head_done, 1)
                if tick == T_GLA - 2:
                    masked(0)
                j, at_ = divmod(tick - T_GLA, GSTEP)
                if 0 <= j < NT:
                    if at_ == 1:
                        for d in range(2):
                            dve.wait_ge(u_done, 20 * h + 2 * j + d + 2)
                            if j == 0:
                                dve.wait_ge(state_zero, h + 2)
                            if j:
                                dve.wait_ge(o_done, 20 * h + 2 * j + 1)
                                dve.wait_ge(s_ready, 20 * h + 2 * j + 1)
                            tile = j if d == 0 else NT - 1 - j
                            after, before = state[:, d, 1 - j % 2, :], state[:, d, j % 2, :]
                            if (d, j) in ((0, TS // P - 1), (1, TP // P - 1)):
                                ins = v_.memset(after, 0.0)
                            else:
                                ins = v_.scalar_tensor_tensor(out=after, in0=before, scalar=ebt[:, d, tile:tile + 1],
                                                              in1=bank[4 + d][:, 0:DV], op0=ALU.mult, op1=ALU.add)
                            ins.then_inc(s_ready, 1)
                    if at_ == 4 and j + 1 < NT:
                        masked(j + 1)
                j, at_ = divmod(tick - T_GLA - 3, GSTEP)
                if 5 <= j < NT and at_ == 0:
                    for d, tile in ((0, j), (1, NT - 1 - j)):
                        dve.wait_ge(o_done, 20 * h + 2 * j + d + 2)
                        if j == 5:
                            dve.wait_ge(go_copied, 10 * h + 11)
                        o = o_gla[:, :, tile * P:tile * P + P]
                        v_.tensor_tensor(o, bank[6 + d][:, 0:DV].rearrange("p (v t) -> p v t", v=2), o, ALU.add
                                         ).then_inc(go_added, 1)

            start = own.base + own.n
            with dve.Fori(0, H) as h:
                own.enter(h, 42)
                dve.wait_ge(head_done, h + 1)
                v_.tensor_copy(slope[:], slopes[:, bass.ds(3 * h, 3)]).then_inc(dve_own, 1)
                dve.wait_ge(dve_own, own.value())
                for tick in range(24 * SLOTS):
                    t, r = divmod(tick, 24)
                    if r == 2:
                        split_low(N_HEAD + t + 1 + h * SLOTS, (N_HEAD + t + 1) % 2)
                    for g in range(3):
                        unit_steps(h, g, tick - 24 * (3 + 3 * g))
                    gla_steps(h, tick)
            own.leave(H, start)

            for j in range(REST):
                split_low(N_REST + j + 1, (N_REST + j + 1) % 2)
            q = 0
            for c, (t0, tw) in enumerate(CHUNKS):
                for k in range(KT):
                    q += 1
                    dve.wait_ge(c_high, q + 1)
                    v_.tensor_tensor(act_lo[:, k, t0:t0 + tw], merged[:, k, t0:t0 + tw],
                                     act_hi[:, k, t0:t0 + tw].bitcast(F32), ALU.subtract).then_inc(c_low, 1)
            for k in range(4):
                q += 1
                dve.wait_ge(c_high, q + 1)
                v_.tensor_tensor(ob_lo[:, k, :], work[:, 4 + k, :], ob_hi[:, k, :].bitcast(F32), ALU.subtract
                                 ).then_inc(c_low, 1)

            def merged_low(c, k):
                t0, tw = CHUNKS[c]
                dve.wait_ge(m_high, c * KT + k + 2)
                v_.tensor_tensor(act_lo[:, k, t0:t0 + tw], merged[:, k, t0:t0 + tw],
                                 act_hi[:, k, t0:t0 + tw].bitcast(F32), ALU.subtract).then_inc(m_low, 1)

            def merge_tile(j, last):
                n = N_C1 + 2 * j
                split_low(n + 1, (N_C1 + 1) % 2, 512)
                for e in range(2):
                    if e == 1:
                        split_low(n + 2, N_C1 % 2)
                    dve.wait_ge(g_sig, 2 * j + e + 2)
                    for c, (t0, tw) in enumerate(CHUNKS):
                        if last and e == 1:
                            for k in range(KT - 1):
                                merged_low(c, k)
                        gate = work[:, 16 + e, t0:t0 + tw]
                        chunk_done(n + e, c)
                        v_.tensor_tensor(gate, bank[c][:, 0:tw], gate, ALU.mult).then_inc(evac, 1)
                        if e == 1:
                            dve.wait_ge(evac, slab_chunks(n + 1) + c + 2)
                            both = merged[:, bass.ds(j, 1), t0:t0 + tw].rearrange("p o t -> p (o t)")
                            v_.tensor_tensor(both, work[:, 16, t0:t0 + tw], gate, ALU.add).then_inc(m_done, 1)
                            if last:
                                merged_low(c, KT - 1)

            with dve.Fori(0, KT - 1) as j:
                merge_tile(j, False)
            merge_tile(KT - 1, True)

            dve.wait_ge(m_low, 3 * KT + 1)
            v_.memset(work[:, 8, :], 0.0).then_inc(x1_acc, 1)
            with dve.Fori(0, KT // 2) as i:
                for e in range(2):
                    split_low(N_C2 + e + 1 + 2 * i, (N_C2 + e + 1) % 2)
                    dve.wait_ge(x1_acc, 2 * i + e + 2)
                    dve.wait_ge(x1_sq, 2 * i + e + 2)
                    v_.tensor_tensor(work[:, 8, :], work[:, 8, :], work[:, 12 + e, :], ALU.add).then_inc(x1_acc, 1)

            def norm_rows(gain, before):
                for c, (t0, tw) in enumerate(CHUNKS):
                    for k in range(KT):
                        dve.wait_ge(n_high, before + c * KT + k + 2)
                        v_.scalar_tensor_tensor(out=act_lo[:, k, t0:t0 + tw], in0=xres[:, k, t0:t0 + tw],
                                                scalar=gain[:, k:k + 1], in1=act_hi[:, k, t0:t0 + tw].bitcast(F32),
                                                op0=ALU.mult, op1=ALU.subtract).then_inc(n_low, 1)

            norm_rows(g_mlp, 0)

            dve.wait_ge(n_r, 2)
            with dve.Fori(0, ROUNDS) as i:
                for e in range(4):
                    n = N_D + e + 4 * i
                    split_low(n + 1, (N_D + e + 1) % 2)
                    for c, (t0, tw) in enumerate(CHUNKS):
                        if e < 2:
                            buf = utmp[:, (3 * e + c) % 2, 0:tw]
                            chunk_done(n, c)
                            v_.scalar_tensor_tensor(out=buf, in0=bank[c][:, 0:tw], scalar=0.0, in1=r_bc[:, t0:t0 + tw],
                                                    op0=ALU.max, op1=ALU.mult).then_inc(evac, 1)
                            dve.wait_ge(u_high, 6 * i + 3 * e + c + 2)
                            v_.tensor_tensor(u_lo[:, e, t0:t0 + tw], buf, u_hi[:, e, t0:t0 + tw].bitcast(F32),
                                             ALU.subtract).then_inc(u_low, 1)
                            continue
                        for jt in range(4):
                            if jt < 3:
                                dve.wait_ge(w2_done, 18 * i + 9 * (e - 2) + 3 * c + jt + 2)
                            else:
                                chunk_done(n, c)
                            x = xres[:, 4 * (e - 2) + jt, t0:t0 + tw]
                            v_.tensor_tensor(x, bank[3 + jt][:, 0:tw], x, ALU.add).then_inc(w2_read if jt < 3 else evac, 1)

            norm_rows(g_ple, 3 * KT)
            for i in range(KT // 2):
                row = 14 + 2 * (i % 2)
                dve.wait_ge(x1_sq, KT + 2 * i + 3)
                v_.tensor_tensor(work[:, row, :], work[:, row, :], work[:, row + 1, :], ALU.add).then_inc(x1_acc, 1)
            for i in range(5):
                dve.wait_ge(p_high, i + 2)
                v_.tensor_tensor(u_lo[:].rearrange("p a t -> p (a t)")[:, 512 * i:512 * i + 512], bank[6 + i % 2][:],
                                 u_hi[:].rearrange("p a t -> p (a t)")[:, 512 * i:512 * i + 512].bitcast(F32),
                                 ALU.subtract).then_inc(p_low, 1)
            dve.wait_ge(n_r, 3)

            def gate_tile(j, last):
                n = N_E + 2 * j
                split_low(n + 1, (N_E + 1) % 2, 256)
                for c, (t0, tw) in enumerate(CHUNKS):
                    row = work[:, 17, t0:t0 + tw]
                    chunk_done(n, c)
                    if c == 0:
                        dve.wait_ge(yt_done, 3 * j + 1)
                    v_.tensor_tensor(row, bank[c][:, 0:tw], r_bc[:, t0:t0 + tw], ALU.mult).then_inc(evac, 1)
                if not last:
                    split_low(n + 2, N_E % 2)
                for c, (t0, tw) in enumerate(CHUNKS):
                    row = work[:, 17, t0:t0 + tw]
                    chunk_done(n + 1, c)
                    dve.wait_ge(pg_sig, 3 * j + c + 2)
                    v_.tensor_tensor(row, bank[c][:, 0:tw], row, ALU.mult).then_inc(evac, 1)
                    dve.wait_ge(evac, slab_chunks(n + 1) + c + 2)
                    x = xres[:, bass.ds(j, 1), t0:t0 + tw].rearrange("p o t -> p (o t)")
                    v_.tensor_tensor(row, x, row, ALU.add).then_inc(y_ready, 1)

            with dve.Fori(0, KT - 1) as j:
                gate_tile(j, False)
            gate_tile(KT - 1, True)


_INS = ["x_prompt", "x_sample", "p_prompt", "p_sample", "norm_mix_g", "w_in", "gla_wa2_f", "gla_ba_f", "gla_wa2_b",
        "gla_ba_b", "gla_norm_g", "attn_qnorm_g", "attn_knorm_g", "w_branch_a", "w_branch_b", "w_out", "norm_mlp_g",
        "w_mlp1", "w_mlp2", "norm_ple_g", "w_ple_gate", "w_ple_proj"]


def kernel(**inputs):
    import numpy as _np
    import concourse.bacc as _bacc
    from concourse import mybir as _mybir
    from concourse.bass_utils import run_bass_kernel_spmd as _run

    nc = _bacc.Bacc("TRN2", target_bir_lowering=False, num_devices=1)
    arrays, aps = {}, {}
    for name in _INS:
        x = _np.ascontiguousarray(inputs[name])
        arrays[f"in_{name}_dram"] = x
        aps[name] = nc.dram_tensor(f"in_{name}_dram", x.shape, _mybir.dt.from_np(x.dtype), kind="ExternalInput").ap()
    outs = []
    for name in ("x_prompt", "x_sample"):
        outs.append(nc.dram_tensor(f"out_{name}_dram", inputs[name].shape, _mybir.dt.float32, kind="ExternalOutput").ap())
    encoder(nc, aps, *outs)
    r = _run(nc, [arrays], core_ids=[0])
    return r.results[0]["out_x_prompt_dram"], r.results[0]["out_x_sample_dram"]
```
